# Optimizing a Trainium2 kernel written in Bass

```python
import math
import jax, jax.numpy as jnp
from jax import lax
import numpy as np

D_MODEL = 1024
BATCH = 1
SEQ = 512
DEPTH = 1
DEC_BATCH = 8
DEC_SEQ = 16
PAST_LEN = 128

CHUNK = 64
ROPE_THETA = 10000.0
NORM_EPS = 1e-6
NEG_INF = -1e30
Q_BLOCK = 128

MLA_HEADS = 8
MLA_NOPE = 64
MLA_ROPE = 32
MLA_V = 64
MLA_QK = MLA_NOPE + MLA_ROPE
Q_LORA = 384
KV_LORA = 256
MLA_SCALE = MLA_QK ** -0.5

SWA_HEADS = 8
SWA_KV_HEADS = 2
SWA_GROUP = SWA_HEADS // SWA_KV_HEADS
SWA_HEAD_DIM = 64
WINDOW = 128
WINDOW_CHUNKS = WINDOW // CHUNK
BAND = (WINDOW_CHUNKS + 1) * CHUNK
SWA_BUF = WINDOW
SWA_SCALE = SWA_HEAD_DIM ** -0.5

N_BRANCH = 2
BRANCH_WIDTH = MLA_HEADS * MLA_V

D_FF = -(-8 * D_MODEL // (3 * 256)) * 256

IN_SPLITS = (Q_LORA, KV_LORA, MLA_ROPE,
             SWA_HEADS * SWA_HEAD_DIM, SWA_KV_HEADS * SWA_HEAD_DIM, SWA_KV_HEADS * SWA_HEAD_DIM,
             N_BRANCH * D_MODEL)
IN_WIDTH = sum(IN_SPLITS)

kernel_name = "chunk_causal_mla_swa_gated_hybrid_step"

def _split(z, sizes):
    outs, start = [], 0
    for s in sizes:
        outs.append(z[..., start:start + s])
        start += s
    return outs

def _rmsnorm(x, g):
    xf = x.astype(jnp.float32)
    y = xf * lax.rsqrt(jnp.mean(xf * xf, axis=-1, keepdims=True) + NORM_EPS)
    return (y * g.astype(jnp.float32)).astype(x.dtype)

def _rope(x, pos):
    half = x.shape[-1] // 2
    inv = ROPE_THETA ** (-jnp.arange(half, dtype=jnp.float32) / half)
    ang = pos.astype(jnp.float32)[:, None] * inv[None, :]
    cos = jnp.cos(ang)[:, None, :]
    sin = jnp.sin(ang)[:, None, :]
    x1 = x[..., :half].astype(jnp.float32)
    x2 = x[..., half:].astype(jnp.float32)
    return jnp.concatenate([x1 * cos - x2 * sin, x2 * cos + x1 * sin], axis=-1).astype(x.dtype)

def _mixer_inputs(h, pos, w_in, g_q, w_uq, g_kv):
    B, T, _ = h.shape
    z = h @ w_in
    q_lat, kv_lat, k_pe, q_s, k_s, v_s, gate_logits = _split(z, IN_SPLITS)
    q = (_rmsnorm(q_lat, g_q) @ w_uq).reshape(B, T, MLA_HEADS, MLA_QK)
    q_mla = jnp.concatenate([q[..., :MLA_NOPE], _rope(q[..., MLA_NOPE:], pos)], axis=-1)
    ckv = _rmsnorm(kv_lat, g_kv)
    kpe = _rope(k_pe[:, :, None, :], pos)[:, :, 0, :]
    q_swa = _rope(q_s.reshape(B, T, SWA_HEADS, SWA_HEAD_DIM), pos)
    k_swa = _rope(k_s.reshape(B, T, SWA_KV_HEADS, SWA_HEAD_DIM), pos)
    v_swa = v_s.reshape(B, T, SWA_KV_HEADS, SWA_HEAD_DIM)
    gates = jax.nn.sigmoid(gate_logits.astype(jnp.float32)).astype(h.dtype).reshape(B, T, N_BRANCH, D_MODEL)
    return q_mla, ckv, kpe, q_swa, k_swa, v_swa, gates

def _mla_kv(ckv, w_ukv):
    kv = jnp.einsum('btc,chd->bthd', ckv, w_ukv)
    return kv[..., :MLA_NOPE], kv[..., MLA_NOPE:]

def _mla_logits(q, k_nope, kpe):
    s = (jnp.einsum('bqhd,bkhd->bhqk', q[..., :MLA_NOPE], k_nope)
         + jnp.einsum('bqhd,bkd->bhqk', q[..., MLA_NOPE:], kpe))
    return s.astype(jnp.float32) * MLA_SCALE

def _mla_prompt(q, ckv, kpe, w_ukv):
    B, S = q.shape[:2]
    k_nope, v = _mla_kv(ckv, w_ukv)
    key_chunk = jnp.arange(S) // CHUNK

    def block(i):
        qb = lax.dynamic_slice_in_dim(q, i * Q_BLOCK, Q_BLOCK, axis=1)
        q_chunk = (i * Q_BLOCK + jnp.arange(Q_BLOCK)) // CHUNK
        mask = key_chunk[None, :] <= q_chunk[:, None]
        s = jnp.where(mask[None, None], _mla_logits(qb, k_nope, kpe), NEG_INF)
        p = jax.nn.softmax(s, axis=-1).astype(v.dtype)
        return jnp.einsum('bhqk,bkhd->bqhd', p, v)

    out = lax.map(block, jnp.arange(S // Q_BLOCK))
    return jnp.transpose(out, (1, 0, 2, 3, 4)).reshape(B, S, MLA_HEADS * MLA_V)

def _mla_sample(q, ckv, kpe, cache_ckv, cache_kpe, w_ukv):
    B, T = q.shape[:2]
    k_nope, v = _mla_kv(jnp.concatenate([cache_ckv, ckv], axis=1), w_ukv)
    kpe_all = jnp.concatenate([cache_kpe, kpe], axis=1)
    p = jax.nn.softmax(_mla_logits(q, k_nope, kpe_all), axis=-1).astype(v.dtype)
    return jnp.einsum('bhqk,bkhd->bqhd', p, v).reshape(B, T, MLA_HEADS * MLA_V)

def _sink_softmax(s, sink):
    m = jnp.maximum(jnp.max(s, axis=-1, keepdims=True), sink)
    e = jnp.exp(s - m)
    return e / (jnp.sum(e, axis=-1, keepdims=True) + jnp.exp(sink - m))

def _swa_prompt(q, k, v, sinks):
    B, S = q.shape[:2]
    NC = S // CHUNK
    qc = q.reshape(B, NC, CHUNK, SWA_KV_HEADS, SWA_GROUP, SWA_HEAD_DIM)

    def band(x):
        xc = x.reshape(B, NC, CHUNK, SWA_KV_HEADS, SWA_HEAD_DIM)
        xp = jnp.concatenate([jnp.zeros((B, WINDOW_CHUNKS, CHUNK, SWA_KV_HEADS, SWA_HEAD_DIM), x.dtype), xc], axis=1)
        return jnp.concatenate([xp[:, j:j + NC] for j in range(WINDOW_CHUNKS + 1)], axis=2)

    kb, vb = band(k), band(v)
    src_chunk = jnp.arange(NC)[:, None] - WINDOW_CHUNKS + jnp.arange(BAND)[None, :] // CHUNK
    valid = src_chunk >= 0
    s = jnp.einsum('bnqgjd,bnkgd->bngjqk', qc, kb).astype(jnp.float32) * SWA_SCALE
    s = jnp.where(valid[None, :, None, None, None, :], s, NEG_INF)
    sink = sinks.astype(jnp.float32).reshape(SWA_KV_HEADS, SWA_GROUP)[:, :, None, None]
    p = _sink_softmax(s, sink).astype(v.dtype)
    o = jnp.einsum('bngjqk,bnkgd->bnqgjd', p, vb).reshape(B, S, SWA_HEADS * SWA_HEAD_DIM)
    return o, k[:, -SWA_BUF:], v[:, -SWA_BUF:]

def _swa_sample(q, k, v, cache_k, cache_v, sinks):
    B, T = q.shape[:2]
    k_all = jnp.concatenate([cache_k, k], axis=1)
    v_all = jnp.concatenate([cache_v, v], axis=1)
    qg = q.reshape(B, T, SWA_KV_HEADS, SWA_GROUP, SWA_HEAD_DIM)
    s = jnp.einsum('btgjd,bkgd->bgjtk', qg, k_all).astype(jnp.float32) * SWA_SCALE
    sink = sinks.astype(jnp.float32).reshape(SWA_KV_HEADS, SWA_GROUP)[:, :, None, None]
    p = _sink_softmax(s, sink).astype(v.dtype)
    o = jnp.einsum('bgjtk,bkgd->btgjd', p, v_all).reshape(B, T, SWA_HEADS * SWA_HEAD_DIM)
    return o, k_all[:, -SWA_BUF:], v_all[:, -SWA_BUF:]

def _layer(x, pos, lw, cache):
    h = _rmsnorm(x, lw['g_pre_mix'])
    q_mla, ckv, kpe, q_swa, k_swa, v_swa, gates = _mixer_inputs(
        h, pos, lw['w_in'], lw['g_q'], lw['w_uq'], lw['g_kv'])
    if cache is None:
        o_mla = _mla_prompt(q_mla, ckv, kpe, lw['w_ukv'])
        o_swa, buf_k, buf_v = _swa_prompt(q_swa, k_swa, v_swa, lw['swa_sinks'])
    else:
        c_ckv, c_kpe, c_k, c_v = cache
        o_mla = _mla_sample(q_mla, ckv, kpe, c_ckv, c_kpe, lw['w_ukv'])
        o_swa, buf_k, buf_v = _swa_sample(q_swa, k_swa, v_swa, c_k, c_v, lw['swa_sinks'])
    branches = jnp.stack([o_mla, o_swa], axis=2)
    proj = jnp.einsum('btnc,ncd->btnd', branches, lw['w_branch'])
    mixed = jnp.sum(gates * proj, axis=2) @ lw['w_out']
    x = x + _rmsnorm(mixed, lw['g_post_mix'])
    h2 = _rmsnorm(x, lw['g_pre_ffn'])
    gu = h2 @ lw['w_gate_up']
    f = (jax.nn.silu(gu[..., :D_FF]) * gu[..., D_FF:]) @ lw['w_down']
    x = x + _rmsnorm(f, lw['g_post_ffn'])
    return x, (ckv, kpe, buf_k, buf_v)

def setup_inputs(seed: int = 0) -> dict:
    key = jax.random.key(seed)
    ks = jax.random.split(key, 24)
    f32 = jnp.float32

    def nrm(k, shape, scale=1.0):
        return jax.random.normal(k, shape, f32) * scale

    def gain(k, dim):
        return 1.0 + 0.1 * jax.random.normal(k, (DEPTH, dim), f32)

    return {
        "x_prompt": nrm(ks[0], (BATCH, SEQ, D_MODEL)),
        "x_sample": nrm(ks[1], (DEC_BATCH, DEC_SEQ, D_MODEL)),
        "cache_mla_ckv": nrm(ks[2], (DEPTH, DEC_BATCH, PAST_LEN, KV_LORA)),
        "cache_mla_kpe": nrm(ks[3], (DEPTH, DEC_BATCH, PAST_LEN, MLA_ROPE)),
        "cache_swa_k": nrm(ks[4], (DEPTH, DEC_BATCH, SWA_BUF, SWA_KV_HEADS, SWA_HEAD_DIM)),
        "cache_swa_v": nrm(ks[5], (DEPTH, DEC_BATCH, SWA_BUF, SWA_KV_HEADS, SWA_HEAD_DIM)),
        "g_pre_mix": gain(ks[6], D_MODEL),
        "w_in": nrm(ks[7], (DEPTH, D_MODEL, IN_WIDTH), D_MODEL ** -0.5),
        "g_q": gain(ks[8], Q_LORA),
        "w_uq": nrm(ks[9], (DEPTH, Q_LORA, MLA_HEADS * MLA_QK), Q_LORA ** -0.5),
        "g_kv": gain(ks[10], KV_LORA),
        "w_ukv": nrm(ks[11], (DEPTH, KV_LORA, MLA_HEADS, MLA_NOPE + MLA_V), KV_LORA ** -0.5),
        "swa_sinks": nrm(ks[12], (DEPTH, SWA_HEADS)),
        "w_branch": nrm(ks[13], (DEPTH, N_BRANCH, BRANCH_WIDTH, D_MODEL), BRANCH_WIDTH ** -0.5),
        "w_out": nrm(ks[14], (DEPTH, D_MODEL, D_MODEL), D_MODEL ** -0.5),
        "g_post_mix": gain(ks[15], D_MODEL),
        "g_pre_ffn": gain(ks[16], D_MODEL),
        "w_gate_up": nrm(ks[17], (DEPTH, D_MODEL, 2 * D_FF), D_MODEL ** -0.5),
        "w_down": nrm(ks[18], (DEPTH, D_FF, D_MODEL), D_FF ** -0.5),
        "g_post_ffn": gain(ks[19], D_MODEL),
    }

def reference(x_prompt, x_sample, cache_mla_ckv, cache_mla_kpe, cache_swa_k, cache_swa_v,
              g_pre_mix, w_in, g_q, w_uq, g_kv, w_ukv, swa_sinks, w_branch, w_out,
              g_post_mix, g_pre_ffn, w_gate_up, w_down, g_post_ffn):
    pos_p = jnp.arange(x_prompt.shape[1])
    pos_s = cache_mla_ckv.shape[2] + jnp.arange(x_sample.shape[1])
    y_prompt, y_sample = x_prompt, x_sample
    pc, pk, pwk, pwv, sc, sk, swk, swv = [], [], [], [], [], [], [], []
    for l in range(DEPTH):
        lw = {
            'g_pre_mix': g_pre_mix[l], 'w_in': w_in[l], 'g_q': g_q[l], 'w_uq': w_uq[l],
            'g_kv': g_kv[l], 'w_ukv': w_ukv[l], 'swa_sinks': swa_sinks[l], 'w_branch': w_branch[l],
            'w_out': w_out[l], 'g_post_mix': g_post_mix[l], 'g_pre_ffn': g_pre_ffn[l],
            'w_gate_up': w_gate_up[l], 'w_down': w_down[l], 'g_post_ffn': g_post_ffn[l],
        }
        y_prompt, (a, b, c, d) = _layer(y_prompt, pos_p, lw, None)
        y_sample, (e, f, g, h) = _layer(
            y_sample, pos_s, lw, (cache_mla_ckv[l], cache_mla_kpe[l], cache_swa_k[l], cache_swa_v[l]))
        pc.append(a); pk.append(b); pwk.append(c); pwv.append(d)
        sc.append(e); sk.append(f); swk.append(g); swv.append(h)
    p_mla_ckv = jnp.stack(pc)
    p_mla_kpe = jnp.stack(pk)
    p_swa_k = jnp.stack(pwk)
    p_swa_v = jnp.stack(pwv)
    s_mla_ckv = jnp.stack(sc)
    s_mla_kpe = jnp.stack(sk)
    s_swa_k = jnp.stack(swk)
    s_swa_v = jnp.stack(swv)
    return (y_prompt, y_sample, p_mla_ckv, p_mla_kpe, p_swa_k, p_swa_v, s_mla_ckv, s_mla_kpe, s_swa_k, s_swa_v)


_drawn_inputs = setup_inputs


def setup_inputs(seed=0):
    import zlib

    import numpy as np

    out = dict(_drawn_inputs(seed))
    spreads = {}
    factors = {'swa_sinks': 8.0}
    for name, (base, spread) in spreads.items():
        noise = np.random.default_rng([zlib.crc32(name.encode()), seed]).standard_normal(out[name].shape)
        drawn = base * np.exp(spread * noise) if base else spread * noise
        out[name] = __import__('jax').numpy.asarray(drawn.astype(out[name].dtype))
    for name, factor in factors.items():
        out[name] = (out[name] * factor).astype(out[name].dtype)
    return out
```

```python
from contextlib import ExitStack

import numpy as np

import concourse.bass as bass
from concourse import mybir

F32 = mybir.dt.float32
F32R = mybir.dt.float32r
BF16 = mybir.dt.bfloat16
ALU = mybir.AluOpType
ACT = mybir.ActivationFunctionType
AX_X = mybir.AxisListType.X

P = 128
D = 1024
SEQ = 512
STREAMS = 8
FRAMES = 16
PAST = 128
CHUNK = 64
TOK = SEQ + STREAMS * FRAMES
TILES = TOK // P
HALF = TOK // 2
KD = D // P
HEADS = 8
NOPE, ROPE, VDIM = 64, 32, 64
QK = NOPE + ROPE
QL, KVL = 384, 256
HD = 64
KV_HEADS = 2
MIX_COLS = 1440
IN_CHUNK = 480
DFF = 2816
KF = DFF // P
EPS = 1e-6
MLA_SCALE = QK ** -0.5
SWA_SCALE = HD ** -0.5
KEYS = PAST + FRAMES

C_KV, C_PE, C_QS, C_KS, C_VS = QL, QL + KVL, QL + KVL + ROPE, 1184, 1312

IN0, G0, G1, BR0, WO0, GU0, DN0 = 0, 12, 20, 28, 36, 44, 88
SLOTS = DN0 + KF

JOBS = (
    [("qlat", t) for t in range(TILES)] + [("ckv", t) for t in range(TILES)] + [("qs", t) for t in range(TILES)]
    + [("uq", n) for n in range(2 * TILES)]
    + [("q", n) for n in range(2 * TILES)] + [("cache", b) for b in range(STREAMS)]
    + [("wuk", n) for n in range(4)] + [("qabs", n) for n in range(4)]
    + [("kt", n) for n in range(4)] + [("v", t) for t in range(4)]
)
JOBS1 = 5 * TILES


def job_engine(kind, n):
    if kind == "qlat":
        return "both"
    if kind == "ckv":
        return "dve"
    if kind == "qs":
        return "act"
    return "act" if n % 2 else "dve"


def job_counts():
    act = dve = 0
    out = []
    for kind, n in JOBS:
        who = job_engine(kind, n)
        act += who != "dve"
        dve += who != "act"
        out.append((act, dve))
    return out


JOB_COUNTS = job_counts()

BLOCKS = (
    [("swa_p", c, g, jp) for c in range(SEQ // CHUNK) for g in range(KV_HEADS) for jp in range(2)]
    + [("swa_s", b, 0, 0) for b in range(STREAMS)]
    + [("mla_s", b, 0, 0) for b in range(STREAMS)]
    + [("mla_p", hp, i, u) for hp in range(HEADS // 2) for i in range(SEQ // P) for u in range(2)]
)


def groups():
    ids, g = [], -1
    last = None
    for kind, a, _, _ in BLOCKS:
        key = (kind, 0 if kind == "swa_s" else a)
        if key != last:
            g += 1
            last = key
        ids.append(g)
    return ids


GROUP = groups()
NB = len(BLOCKS)
FIRST_OF = [n == 0 or GROUP[n - 1] != GROUP[n] for n in range(NB)]
LAST_OF = [n == NB - 1 or GROUP[n + 1] != GROUP[n] for n in range(NB)]
GROUP_KIND = {GROUP[n]: BLOCKS[n][0] for n in range(NB)}
NGROUPS = GROUP[-1] + 1


def lo_groups(upto):
    return sum(GROUP_KIND[g] != "mla_s" for g in range(upto))


def window(c):
    base = max(0, (c // 2 - 1)) * P
    return base, max(0, c - 2) * CHUNK - base, (c + 1) * CHUNK - base


def n_keys(block):
    kind, a, b, _ = block
    if kind == "swa_p":
        return window(a)[2]
    if kind == "mla_p":
        return (b + 1) * P
    return KEYS


def rope_tables():
    half = HD // 2
    inv = np.float32(10000.0) ** (-np.arange(half, dtype=np.float32) / np.float32(half))
    pos = np.concatenate([np.arange(SEQ), PAST + np.arange(STREAMS * FRAMES) % FRAMES]).astype(np.float32)
    ang = (pos[:, None] * inv[None, :].astype(np.float32)).astype(np.float32)
    shape = lambda a: np.ascontiguousarray(
        a.astype(np.float32).reshape(TILES, P, half).transpose(1, 0, 2).reshape(P, TILES * half))
    return shape(np.cos(ang)), shape(np.sin(ang))


def build_layer(nc, x_prompt, x_sample, cache_mla_ckv, cache_mla_kpe, cache_swa_k, cache_swa_v,
                g_pre_mix, w_in, g_q, w_uq, g_kv, w_ukv, swa_sinks, w_branch, w_out,
                g_post_mix, g_pre_ffn, w_gate_up, w_down, g_post_ffn,
                y_prompt, y_sample, p_ckv, p_kpe, p_k, p_v, s_ckv, s_kpe, s_k, s_v):
    cos_np, sin_np = rope_tables()
    cos_dram = nc.inline_tensor(cos_np, "rope_cos").ap()
    sin_dram = nc.inline_tensor(sin_np, "rope_sin").ap()
    gates_dram = nc.dram_tensor("gates_scratch", (16, P, TOK), F32, kind="Internal").ap()
    x1_dram = nc.dram_tensor("x1_scratch", (P, TILES, D), F32, kind="Internal").ap()

    win_v = w_in[0].rearrange("(k p) n -> p k n", p=P)
    wbr_v = w_branch[0].rearrange("b (t p) n -> p (b t) n", p=P)
    wout_v = w_out[0].rearrange("(k p) n -> p k n", p=P)
    wgu_v = w_gate_up[0].rearrange("(k p) n -> p k n", p=P)
    wdn_v = w_down[0].rearrange("(k p) n -> p k n", p=P)

    def x_rows(t):
        return x_prompt[0, t * P:(t + 1) * P, :] if t < 4 else x_sample.rearrange("b t d -> (b t) d")

    def y_rows(t):
        return y_prompt[0, t * P:(t + 1) * P, :] if t < 4 else y_sample.rearrange("b t d -> (b t) d")

    SB0 = 16512

    def at(name, shape, word, dt=F32):
        return nc.alloc_sbuf_tensor_at(name, shape, dt, offset=SB0 + 4 * word)

    raw = at("raw", [P, 4, 1024], 0)
    whi = at("whi", [P, 2, 1024], 4096, F32R)
    wlo = at("wlo", [P, 2, 1024], 6144, F32R)
    ident = at("ident", [P, P], 8192)
    cos_t = at("cos_t", [P, TILES, 32], 8320)
    sin_t = at("sin_t", [P, TILES, 32], 8480)
    gq_b = at("gq_b", [P, QL], 8640)
    gkv_b = at("gkv_b", [P, KVL], 9024)
    ssq_h = at("ssq_h", [P, 8], 9280)
    sd_h = at("sd_h", [P, 8], 9288)
    r_h = at("r_h", [P, 8], 9296)
    ssq_z = at("ssq_z", [P, 2, 8], 9304)
    sd_z = at("sd_z", [P, 2, 8], 9320)
    r_z = at("r_z", [P, 2, 8], 9336)
    mx_c = at("mx_c", [P, 8], 9352)
    nm_c = at("nm_c", [P, 8], 9360)
    sum_c = at("sum_c", [P, 8], 9368)
    inv_c = at("inv_c", [P, 8], 9376)
    es_c = at("es_c", [P, 8], 9384)
    den_c = at("den_c", [P, 8], 9392)
    sink_b = at("sink_b", [P, 8], 9400)
    sink_c = at("sink_c", [P, 8], 9408)
    nsink_c = at("nsink_c", [P, 8], 9416)
    eps_c = at("eps_c", [P, 8], 9424)
    mask_q = at("mask_q", [1, P], 9432, BF16)
    mask_k = at("mask_k", [1, P], 9496, BF16)
    ssq_a = at("ssq_a", [P, 2, 8], 9560)
    rs_a = at("rs_a", [P, 3, 8], 9576)

    def area(name, shape, word, dt=F32):
        return at(name, shape, 9600 + word, dt)

    h_hi = area("h_hi", [P, KD, TOK], 0, F32R)
    h_lo = area("h_lo", [P, KD, TOK], 5120, F32R)
    x_t = area("x_t", [P, TILES, D], 10240)
    junk_h = area("junk_h", [P, D], 27680)
    gpre_b = area("gpre_b", [P, D], 42400)
    ql_hi = area("ql_hi", [P, 3, TOK], 10240, F32R)
    ql_lo = area("ql_lo", [P, 3, TOK], 12160, F32R)
    wuq_hi = area("wuq_hi", [P, 3, 768], 15360, F32R)
    wuq_lo = area("wuq_lo", [P, 3, 768], 17664, F32R)
    wuq_raw = area("wuq_raw", [P, 3, 768], 37536)
    z = area("z", [P, TILES, MIX_COLS], 20480)
    rope_a = area("rope_a", [P, TILES, 10, 32], 35488)
    rope_b = area("rope_b", [P, TILES, 10, 32], 37088)
    rope_c = area("rope_c", [P, TILES, 10, 32], 38688)
    rope_d = area("rope_d", [P, TILES, 10, 32], 40288)
    gate_s = area("gate_s", [P, 2, TOK], 14080)
    q_t = area("q_t", [P, TILES, HEADS, QK], 20480)
    qro_a = area("qro_a", [P, TILES, HEADS, 16], 10240)
    qro_b = area("qro_b", [P, TILES, HEADS, 16], 10880)
    qro_c = area("qro_c", [P, TILES, HEADS, 16], 11520)
    qro_d = area("qro_d", [P, TILES, HEADS, 16], 12160)
    qs_T = area("qs_T", [P, SEQ // CHUNK, 4, CHUNK], 27680)
    qs_Ts = area("qs_Ts", [P, STREAMS, 4, FRAMES], 29728)
    ks_T = area("ks_T", [P, TOK], 30240)
    v_s = area("v_s", [P, TILES, P], 30880)
    ckv_T = area("ckv_T", [P, 2, TOK], 31520)
    kpe_T = area("kpe_T", [P, TOK], 32800)
    w_uk = area("w_uk", [P, 2, HEADS, NOPE], 33440)
    w_uv = area("w_uv", [P, 2, HEADS, VDIM], 34464)
    wuk_T = area("wuk_T", [64, HEADS, KVL], 35488)
    olat = area("olat", [P, 2, HEADS, P], 35488)
    ckv_Ta = area("ckv_Ta", [P, 2, STREAMS, KEYS], 37536)
    kpe_Ta = area("kpe_Ta", [P, STREAMS, KEYS], 39840)
    k_Ta = area("k_Ta", [P, STREAMS, KEYS], 40992)
    c_kpe = area("c_kpe", [P, STREAMS, ROPE], 42144)
    c_v = area("c_v", [P, STREAMS, P], 42400)
    c_ckv = area("c_ckv", [P, STREAMS, KVL], 15360)
    ckv_new = area("ckv_new", [FRAMES, STREAMS, KVL], 17408)
    c_k = area("c_k", [P, STREAMS, P], 19456)
    q_T = area("q_T", [P, HEADS, SEQ], 0)
    q_Ts = area("q_Ts", [P, STREAMS, HEADS, FRAMES], 4096)
    k_T = area("k_T", [P, HEADS, SEQ], 5120)
    v_new = area("v_new", [FRAMES, STREAMS, P], 9216)
    v_p = area("v_p", [P, 4, SEQ], 20480)
    qabs = area("qabs", [P, 2, STREAMS, HEADS, FRAMES], 22528)
    probs = area("probs", [P, 3, 512], 25120)
    probs_T = area("probs_T", [P, 2, 512], 26656)
    os_hi = area("os_hi", [P, 4, TOK], 10240, F32R)
    os_lo = area("os_lo", [P, 4, TOK], 12800, F32R)
    om_hi = area("om_hi", [P, 4, TOK], 15360, F32R)
    om_lo = area("om_lo", [P, 4, TOK], 17920, F32R)
    gate_r = area("gate_r", [P, 2, 2, TOK], 27680)
    mix_a = area("mix_a", [P, TOK], 30240)
    mix_b = area("mix_b", [P, TOK], 30880)
    mix_s = area("mix_s", [P, 2, TOK], 31520)
    m_hi = area("m_hi", [P, KD, TOK], 0, F32R)
    m_lo = area("m_lo", [P, KD, TOK], 5120, F32R)
    x1 = area("x1", [P, TILES, D], 10240)
    x_r = area("x_r", [P, TILES, D], 15360)
    gpm_b = area("gpm_b", [P, D], 20480)
    gpf_b = area("gpf_b", [P, D], 21504)
    h2n = area("h2n", [P, 2, D], 22528)
    junk_m = area("junk_m", [P, D], 24576)
    h2_hi = area("h2_hi", [P, KD, TOK], 33296, F32R)
    h2_lo = area("h2_lo", [P, KD, TOK], 38416, F32R)
    gu_hi = area("gu_hi", [P, KF, TOK], 0, F32R)
    gu_lo = area("gu_lo", [P, KF, TOK], KF * TOK, F32R)
    silu_s = area("silu_s", [P, 2, TOK], 28160)
    gu_s = area("gu_s", [P, 2, TOK], 29440)
    gpo_b = area("gpo_b", [P, D], 30720)
    junk_f = area("junk_f", [P, D], 31744)
    f_t = area("f_t", [P, TILES, D], 33296)
    x1_r = area("x1_r", [P, TILES, D], 38416)

    with ExitStack() as ctx:
        ps = ctx.enter_context(nc.psum_tensor("ps", [P, 8, 512], F32))

        def sem(name):
            return ctx.enter_context(nc.semaphore(name))

        x_in = [sem(f"x_in{t}") for t in range(TILES)]
        gpre_in, tab_in, wuq_in, wukv_in, sink_in = (sem(n) for n in ("gpre_in", "tab_in", "wuq_in", "wukv_in", "sink_in"))
        w_raw = [sem(f"w_raw{r}") for r in range(4)]
        w_hi, w_lo, w_used = sem("w_hi"), sem("w_lo"), sem("w_used")
        const_rdy, sink_rdy = sem("const_rdy"), sem("sink_rdy")
        h_ssq, h_sd, h_rs, h_norm, h_tr, h_hi_rdy = (sem(n) for n in ("h_ssq", "h_sd", "h_rs", "h_norm", "h_tr", "h_hi_rdy"))
        bank_empty = sem("bank_empty")
        z_mm = sem("z_mm")
        z_ssq, z_sd, z_rs = sem("z_ssq"), sem("z_sd"), sem("z_rs")
        pool_step, z_rdy, z_st, v_s_rdy = sem("pool_step"), sem("z_rdy"), sem("z_st"), sem("v_s_rdy")
        wuq_rdy, q_rdy, tails_rdy = sem("wuq_rdy"), sem("q_rdy"), sem("tails_rdy")
        g_sig = sem("g_sig")
        g_st = [sem("g_st0"), sem("g_st1")]
        job_full, job_act, job_dve = sem("job_full"), sem("job_act"), sem("job_dve")
        kpe_rdy = sem("kpe_rdy")
        cache_in, new_in = sem("cache_in"), sem("new_in")
        s_full, s_max, s_nm, s_exp, s_es, s_den, s_inv, s_norm = (
            sem(n) for n in ("s_full", "s_max", "s_nm", "s_exp", "s_es", "s_den", "s_inv", "s_norm"))
        pt_full, pt_rdy, pv_done, o_hi, o_lo = (
            sem(n) for n in ("pt_full", "pt_rdy", "pv_done", "o_hi", "o_lo"))
        g_ld = [sem("g_ld0"), sem("g_ld1")]
        b_prod, b_sum, b_hi, b_lo = sem("b_prod"), sem("b_sum"), sem("b_hi"), sem("b_lo")
        wo_in, wo_mm = sem("wo_in"), sem("wo_mm")
        m_ssq, m_tot, m_sd, m_rs, m_sc, x1_rdy, x1_st = (
            sem(n) for n in ("m_ssq", "m_tot", "m_sd", "m_rs", "m_sc", "x1_rdy", "x1_st"))
        h2_ssq, h2_sd, h2_rs, h2_norm, h2_tr, h2_hi_rdy = (
            sem(n) for n in ("h2_ssq", "h2_sd", "h2_rs", "h2_norm", "h2_tr", "h2_hi_rdy"))
        gpo_in, x1_in = sem("gpo_in"), sem("x1_in")
        u_silu, u_prod, u_hi, u_lo = sem("u_silu"), sem("u_prod"), sem("u_hi"), sem("u_lo")
        f_mm, f_ssq, f_tot, f_sd, f_rs, f_sc, y_rdy, y_st = (
            sem(n) for n in ("f_mm", "f_ssq", "f_tot", "f_sd", "f_rs", "f_sc", "y_rdy", "y_st"))

        block = ctx.enter_context(nc.Block())

        def job_emptied(eng, j):
            who = job_engine(*JOBS[j])
            act, dve = JOB_COUNTS[j]
            if who == "act":
                eng.wait_ge(job_act, act)
            else:
                eng.wait_ge(job_dve, dve)

        def job_index(kind, n):
            return JOBS.index((kind, n))

        def rope_out(eng, base, x1v, x2v, cosv, sinv, ta, tb, tc, td, outs):
            eng.tensor_tensor(ta, x1v, cosv, ALU.mult).then_inc(pool_step, 1)
            eng.tensor_tensor(tb, x2v, sinv, ALU.mult).then_inc(pool_step, 1)
            eng.tensor_tensor(tc, x2v, cosv, ALU.mult).then_inc(pool_step, 1)
            eng.tensor_tensor(td, x1v, sinv, ALU.mult).then_inc(pool_step, 1)
            eng.wait_ge(pool_step, base + 4)
            for part, x1o, x2o in outs:
                eng.tensor_tensor(x1o, part(ta), part(tb), ALU.subtract).then_inc(pool_step, 1)
                eng.tensor_tensor(x2o, part(tc), part(td), ALU.add).then_inc(pool_step, 1)
            eng.wait_ge(pool_step, base + 4 + 2 * len(outs))
            return base + 4 + 2 * len(outs)

        def job_copies(kind, n, bank):
            if kind == "ckv":
                c = slice(n * P, (n + 1) * P)
                return [(ckv_T[:, :, c], bank[:, 0:256].rearrange("p (k n) -> p k n", k=2)), (ks_T[:, c], bank[:, 256:384]),
                        (kpe_T[64:96, c], bank[0:32, 384:512])]
            if kind == "qs":
                if n == 4:
                    return [(qs_Ts[:], bank.rearrange("p (i b t) -> p b i t", i=4, b=STREAMS))]
                return [(qs_T[:, 2 * n:2 * n + 2], bank.rearrange("p (i c n) -> p c i n", i=4, c=2))]
            if kind == "uq":
                t, half = divmod(n, 2)
                return [(q_t[:, t, 4 * half:4 * half + 4, :], bank[:, 0:384].rearrange("p (h n) -> p h n", h=4))]
            if kind == "q":
                t, half = divmod(n, 2)
                h4 = slice(4 * half, 4 * half + 4)
                if t == 4:
                    return [(q_Ts[0:QK, :, h4, :], bank[0:QK, :].rearrange("p (h b t) -> p b h t", h=4, b=STREAMS))]
                return [(q_T[0:QK, h4, t * P:(t + 1) * P], bank[0:QK, :].rearrange("p (h n) -> p h n", h=4))]
            if kind == "cache":
                return [(ckv_Ta[:, :, n, 0:PAST], bank[:, 0:256].rearrange("p (k n) -> p k n", k=2)),
                        (k_Ta[:, n, 0:PAST], bank[:, 256:384]), (kpe_Ta[64:96, n, 0:PAST], bank[0:32, 384:512])]
            if kind == "wuk":
                return [(wuk_T[:, 2 * n:2 * n + 2, :], bank[0:64, :].rearrange("p (h n) -> p h n", h=2))]
            if kind == "qabs":
                ct, half = divmod(n, 2)
                return [(qabs[:, ct, :, 4 * half:4 * half + 4, :],
                         bank.rearrange("p (h b t) -> p b h t", h=4, b=STREAMS))]
            if kind == "kt":
                return [(k_T[0:NOPE, 2 * n, :], bank[0:64, :]), (k_T[0:NOPE, 2 * n + 1, :], bank[64:128, :])]
            return [(v_p[:, n, :], bank[:, :])]

        def o_copies(k, hi):
            kind, a, _, _ = BLOCKS[k]
            bank = ps[:, 5 + GROUP[k] % 2, :]
            o_s = os_hi if hi else os_lo
            o_m = om_hi if hi else om_lo
            if kind == "swa_p":
                return [(o_s[:, :, a * CHUNK:(a + 1) * CHUNK], bank[:, 0:256].rearrange("p (j n) -> p j n", j=4))]
            if kind == "swa_s":
                v = bank.rearrange("p (j n) -> p j n", j=4)
                return [(o_s[64 * par:64 * par + 64, 2 * g:2 * g + 2, SEQ:TOK], v[64 * g:64 * g + 64, par:4:2, :])
                        for g in range(2) for par in range(2)]
            if kind == "mla_s":
                return [(olat[:, :, :, a * FRAMES:(a + 1) * FRAMES],
                         bank[:, 0:256].rearrange("p (c h t) -> p c h t", c=2, h=HEADS))]
            return [(o_m[:, a, 0:SEQ], bank[:, :])]

        @block.sync
        def _(sp):
            def load(r, src, width):
                dst = raw[:, r, 0:8 * 128] if width == 128 else raw[:, r, 0:2 * width]
                sp.dma_start(dst.rearrange("p (k n) -> p k n", n=width), src).then_inc(w_raw[r], 16)

            for t in range(TILES):
                sp.dma_start(x_t[:, t, :], x_rows(t)).then_inc(x_in[t], 16)
            for j in range(4):
                load(j, win_v[:, 2 * j:2 * j + 2, 0:IN_CHUNK], IN_CHUNK)
            with sp.Fori(0, 2) as it:
                for j in range(4):
                    sp.wait_ge(w_lo, it * 4 + (j + 1))
                    load(j, win_v[:, 2 * j:2 * j + 2, bass.ds(it * IN_CHUNK + IN_CHUNK, IN_CHUNK)], IN_CHUNK)
            for j in range(4):
                sp.wait_ge(w_lo, 8 + j + 1)
                load(j, win_v[:, :, MIX_COLS + j * P:MIX_COLS + (j + 1) * P], P)
            with sp.Fori(0, 3) as it:
                for j in range(4):
                    sp.wait_ge(w_lo, it * 4 + (G0 + j + 1))
                    load(j, win_v[:, :, bass.ds(it * 512 + (MIX_COLS + (4 + j) * P), P)], P)
                    sp.wait_ge(g_sig, it * 4 + (j + 1))
                    sp.dma_start(gates_dram[bass.ds(it * 4 + j, 1)].rearrange("a p n -> (a p) n"),
                                 gate_s[:, j % 2, :]).then_inc(g_st[j % 2], 16)
            sp.wait_ge(job_full, JOBS1)
            sp.dma_start(c_ckv[:], cache_mla_ckv[0].rearrange("b s c -> s b c")).then_inc(cache_in, 16)
            sp.dma_start(c_k[:], cache_swa_k[0].rearrange("b s g d -> s b (g d)")).then_inc(cache_in, 16)
            sp.dma_start(c_v[:], cache_swa_v[0].rearrange("b s g d -> s b (g d)")).then_inc(cache_in, 16)
            sp.dma_start(c_kpe[:], cache_mla_kpe[0].rearrange("b s c -> s b c")).then_inc(cache_in, 16)
            for j in range(4):
                sp.wait_ge(w_lo, G1 + 4 + j + 1)
                load(j, wbr_v[:, :, j * P:(j + 1) * P], P)
                sp.wait_ge(g_sig, 12 + j + 1)
                sp.dma_start(gates_dram[12 + j], gate_s[:, j % 2, :]).then_inc(g_st[j % 2], 16)
            sp.wait_ge(z_st, 16 * 24)
            sp.wait_ge(w_used, BR0)
            sp.dma_start(ckv_new[:], s_ckv[0].rearrange("b t c -> t b c")).then_inc(new_in, 16)
            sp.dma_start(v_new[:], s_v[0, :, PAST - FRAMES:PAST].rearrange("b t g d -> t b (g d)")).then_inc(new_in, 16)
            sp.wait_ge(pv_done, NB)
            sp.wait_ge(g_st[0], 16 * 8)
            sp.wait_ge(g_st[1], 16 * 8)
            gates_v = gates_dram.rearrange("(b m) p n -> m p b n", b=2)
            for m in range(2):
                sp.dma_start(gate_r[:, m], gates_v[m]).then_inc(g_ld[m], 16)
            for m in range(8):
                sp.wait_ge(w_lo, BR0 + m + 1)
                if m < 4:
                    load(m % 4, wbr_v[:, :, (m + 4) * P:(m + 5) * P], P)
                else:
                    load(m % 4, wout_v[:, 2 * (m - 4):2 * (m - 4) + 2, 0:512], 512)
                if m < 6:
                    sp.wait_ge(b_prod, 2 * (m + 1))
                    sp.dma_start(gate_r[:, m % 2], gates_v[m + 2]).then_inc(g_ld[m % 2], 16)
            sp.wait_ge(w_used, WO0)
            sp.wait_ge(b_lo, 8)
            for t in range(TILES):
                sp.dma_start(x_r[:, t, :], x_rows(t)).then_inc(wo_in, 16)
            sp.dma_start(gpm_b[:], g_post_mix.to_broadcast([P, D])).then_inc(wo_in, 16)
            sp.dma_start(gpf_b[:], g_pre_ffn.to_broadcast([P, D])).then_inc(wo_in, 16)
            for j in range(4):
                sp.wait_ge(w_lo, WO0 + j + 1)
                load(j, wout_v[:, 2 * j:2 * j + 2, 512:1024], 512)
            for j in range(4):
                sp.wait_ge(w_lo, WO0 + 4 + j + 1)
                load(j, wgu_v[:, :, (j // 2) * P + (j % 2) * DFF:(j // 2 + 1) * P + (j % 2) * DFF], P)
            for t in range(TILES):
                sp.wait_ge(x1_rdy, t + 1)
                sp.dma_start(x1_dram[:, t, :], x1[:, t, :]).then_inc(x1_st, 16)
            with sp.Fori(0, 10) as it:
                for j in range(4):
                    sp.wait_ge(w_lo, it * 4 + (GU0 + j + 1))
                    load(j, wgu_v[:, :, bass.ds(it * 256 + (256 + (j // 2) * P + (j % 2) * DFF), P)], P)
            for j in range(4):
                sp.wait_ge(w_lo, GU0 + 40 + j + 1)
                load(j, wdn_v[:, 2 * j:2 * j + 2, 0:512], 512)
            sp.dma_start(gpo_b[:], g_post_ffn.to_broadcast([P, D])).then_inc(gpo_in, 16)
            for u in range(KF - 4):
                if u == 1:
                    sp.wait_ge(w_used, DN0)
                    sp.wait_ge(x1_st, 16 * TILES)
                    sp.dma_start(x1_r[:], x1_dram).then_inc(x1_in, 16)
                sp.wait_ge(w_lo, DN0 + u + 1)
                half, k = divmod(u + 4, KF // 2)
                load(u % 4, wdn_v[:, 2 * k:2 * k + 2, half * 512:(half + 1) * 512], 512)
            for t in range(TILES):
                sp.wait_ge(y_rdy, t + 1)
                sp.dma_start(y_rows(t), f_t[:, t, :]).then_inc(y_st, 16)
            sp.wait_ge(y_st, 16 * TILES)

        @block.gpsimd
        def _(pool):
            pool.memset(ident[:], 0.0).then_inc(pool_step, 1)
            pool.memset(mask_q[:], 0.0).then_inc(pool_step, 1)
            pool.memset(mask_k[:], 0.0).then_inc(pool_step, 1)
            pool.memset(raw[:, :, 960:1024], 0.0).then_inc(pool_step, 1)
            pool.memset(eps_c[:], EPS).then_inc(pool_step, 1)
            pool.wait_ge(pool_step, 5)
            pool.memset(mask_q[:, 0:CHUNK], 1.0).then_inc(const_rdy, 1)
            pool.memset(mask_k[:, CHUNK:P], -1e30).then_inc(const_rdy, 1)
            pool.affine_select(out=ident[:], in_=ident[:], compare_op=ALU.not_equal, fill=1.0, base=0,
                               pattern=[[-1, P]], channel_multiplier=1).then_inc(const_rdy, 1)
            pool.wait_ge(wuq_in, 16)
            pool.tensor_copy(wuq_hi[:], wuq_raw[:]).then_inc(pool_step, 1)
            pool.wait_ge(pool_step, 6)
            pool.tensor_tensor(wuq_lo[:], wuq_raw[:], wuq_hi[:].bitcast(F32), ALU.subtract).then_inc(wuq_rdy, 1)
            pool.wait_ge(wuq_rdy, 1)
            pool.wait_ge(sink_in, 16 * 9)
            for u in range(2):
                pool.tensor_copy(sink_c[64 * u:64 * u + 64, 0:4], sink_b[64 * u:64 * u + 64, u:8:2]).then_inc(pool_step, 1)
            pool.wait_ge(pool_step, 8)
            pool.tensor_scalar(nsink_c[:, 0:5], sink_c[:, 0:5], -1.0, None, ALU.mult).then_inc(sink_rdy, 1)
            pool.wait_ge(bank_empty, 25)
            pool.wait_ge(tab_in, 16 * 4)
            pool.tensor_copy(v_s[:], z[:, :, C_VS:MIX_COLS]).then_inc(v_s_rdy, 1)
            qk = z[:, :, C_QS:C_VS].rearrange("p t (h d) -> p t h d", d=HD)
            pairs = z[:, :, C_QS:C_KS].rearrange("p t (i g d) -> p t i g d", i=4, g=2)
            qk_outs = [(lambda v, g=g: v[:, :, 4 * g:4 * g + 4, :], pairs[:, :, :, g, 0:32], pairs[:, :, :, g, 32:64])
                       for g in range(2)]
            qk_outs.append((lambda v: v[:, :, 8:10, :], qk[:, :, 8:10, 0:32], qk[:, :, 8:10, 32:64]))
            cos_b = cos_t[:].unsqueeze(2).to_broadcast([P, TILES, 10, 32])
            sin_b = sin_t[:].unsqueeze(2).to_broadcast([P, TILES, 10, 32])
            n = rope_out(pool, 8, qk[:, :, :, 0:32], qk[:, :, :, 32:64], cos_b, sin_b,
                         rope_a[:], rope_b[:], rope_c[:], rope_d[:], qk_outs)
            pe_v = z[:, :, C_PE:C_QS]
            n = rope_out(pool, n, pe_v[:, :, 0:16], pe_v[:, :, 16:32], cos_t[:, :, 0:32:2], sin_t[:, :, 0:32:2],
                         rope_a[:, :, 0, 0:16], rope_b[:, :, 0, 0:16], rope_c[:, :, 0, 0:16], rope_d[:, :, 0, 0:16],
                         [(lambda v: v, pe_v[:, :, 0:16], pe_v[:, :, 16:32])])
            pool.wait_ge(z_rs, 2)
            for i, (lo, width, g_b) in enumerate(((0, QL, gq_b), (QL, KVL, gkv_b))):
                part = z[:, :, lo:lo + width]
                pool.tensor_tensor(part, part, r_z[:, i, 0:TILES].unsqueeze(2).to_broadcast([P, TILES, width]),
                                   ALU.mult).then_inc(pool_step, 1)
                pool.wait_ge(pool_step, n + 1)
                pool.tensor_tensor(part, part, g_b[:].unsqueeze(1).to_broadcast([P, TILES, width]),
                                   ALU.mult).then_inc(pool_step, 1)
                n += 2
            pool.wait_ge(pool_step, n)
            pool.tensor_copy(rope_a[:, 0, 0, 0:1], cos_t[:, 0, 0:1]).then_inc(z_rdy, 1)
            def out(dst, src):
                pool.dma_start(dst, src).then_inc(z_st, 16)

            out(p_ckv[0, 0].rearrange("(t p) c -> p t c", p=P), z[:, 0:4, C_KV:C_PE])
            out(s_ckv[0].rearrange("b t c -> (b t) c"), z[:, 4, C_KV:C_PE])
            out(p_kpe[0, 0].rearrange("(t p) c -> p t c", p=P), z[:, 0:4, C_PE:C_QS])
            out(s_kpe[0].rearrange("b t c -> (b t) c"), z[:, 4, C_PE:C_QS])
            out(p_k[0, 0].rearrange("s g d -> s (g d)"), z[:, 3, C_KS:C_VS])
            out(p_v[0, 0].rearrange("s g d -> s (g d)"), z[:, 3, C_VS:MIX_COLS])
            for b in range(STREAMS):
                rows = slice(b * FRAMES, (b + 1) * FRAMES)
                out(s_k[0, b, PAST - FRAMES:PAST].rearrange("s g d -> s (g d)"), z[rows, 4, C_KS:C_VS])
                out(s_v[0, b, PAST - FRAMES:PAST].rearrange("s g d -> s (g d)"), z[rows, 4, C_VS:MIX_COLS])
            out(s_k[0, :, 0:PAST - FRAMES], cache_swa_k[0, :, FRAMES:PAST])
            out(s_v[0, :, 0:PAST - FRAMES], cache_swa_v[0, :, FRAMES:PAST])
            job_emptied(pool, JOBS1 - 1)
            job_emptied(pool, JOBS1 - 2)
            cos_q = cos_t[:, :, 0:32:2].unsqueeze(2).to_broadcast([P, TILES, HEADS, 16])
            sin_q = sin_t[:, :, 0:32:2].unsqueeze(2).to_broadcast([P, TILES, HEADS, 16])
            n = rope_out(pool, n, q_t[:, :, :, NOPE:NOPE + 16], q_t[:, :, :, NOPE + 16:QK], cos_q, sin_q,
                         qro_a[:], qro_b[:], qro_c[:], qro_d[:],
                         [(lambda v: v, q_t[:, :, :, NOPE:NOPE + 16], q_t[:, :, :, NOPE + 16:QK])])
            pool.tensor_copy(eps_c[:, 1:2], eps_c[:, 0:1]).then_inc(q_rdy, 1)
            for ct in range(2):
                pool.tensor_copy(ckv_Ta[:, ct, :, PAST:KEYS],
                                 ckv_T[:, ct, SEQ:TOK].rearrange("p (b t) -> p b t", t=FRAMES)).then_inc(tails_rdy, 1)
            pool.tensor_copy(k_Ta[:, :, PAST:KEYS], ks_T[:, SEQ:TOK].rearrange("p (b t) -> p b t", t=FRAMES)).then_inc(tails_rdy, 1)
            pool.wait_ge(tails_rdy, 3)
            pool.tensor_copy(kpe_Ta[64:96, :, PAST:KEYS],
                             kpe_T[64:96, SEQ:TOK].rearrange("p (b t) -> p b t", t=FRAMES)).then_inc(tails_rdy, 1)
            pool.wait_ge(z_st, 16 * 24)

        @block.scalar
        def _(act):
            act.dma_start(gpre_b[:], g_pre_mix.to_broadcast([P, D])).then_inc(gpre_in, 16)
            act.dma_start(wuq_raw[:], w_uq[0].rearrange("(k p) n -> p k n", p=P)).then_inc(wuq_in, 16)
            act.dma_start(cos_t[:], cos_dram.rearrange("p (t c) -> p t c", t=TILES)).then_inc(tab_in, 16)
            act.dma_start(sin_t[:], sin_dram.rearrange("p (t c) -> p t c", t=TILES)).then_inc(tab_in, 16)
            act.dma_start(gq_b[:], g_q.to_broadcast([P, QL])).then_inc(tab_in, 16)
            act.dma_start(gkv_b[:], g_kv.to_broadcast([P, KVL])).then_inc(tab_in, 16)
            for k in range(2):
                act.dma_start(w_uk[:, k], w_ukv[0, k * P:(k + 1) * P, :, 0:NOPE]).then_inc(wukv_in, 16)
                act.dma_start(w_uv[:, k], w_ukv[0, k * P:(k + 1) * P, :, NOPE:NOPE + VDIM]).then_inc(wukv_in, 16)
            act.dma_start(sink_b[:], swa_sinks.to_broadcast([P, HEADS])).then_inc(sink_in, 16)
            for h in range(HEADS):
                act.dma_start(sink_c[h * FRAMES:(h + 1) * FRAMES, 4:5],
                              swa_sinks[:, h:h + 1].to_broadcast([FRAMES, 1])).then_inc(sink_in, 16)

            def split_hi(s, r, arrived):
                act.wait_ge(w_raw[r], arrived)
                act.activation(whi[:, r % 2, :], raw[:, r, :], ACT.Copy).then_inc(w_hi, 1)

            def after_slot(base, it, j):
                s = it * 4 + (base + j)
                act.wait_ge(w_used, s + 1)
                r = (base + j + 2) % 4
                split_hi(s, r, it * 16 + 16 * ((base + j + 2) // 4 + 1))

            act.wait_ge(const_rdy, 3)
            for t in range(TILES):
                act.wait_ge(x_in[t], 16)
                if t:
                    act.wait_ge(h_ssq, t)
                act.activation(junk_h[:], x_t[:, t, :], ACT.Square, accum_out=ssq_h[:, t:t + 1]).then_inc(h_ssq, 1)
                act.wait_ge(h_ssq, t + 1)
                act.activation(sd_h[:, t:t + 1], ssq_h[:, t:t + 1], ACT.Sqrt, scale=1.0 / D,
                               bias=eps_c[:, 0:1]).then_inc(h_sd, 1)
            split_hi(0, 0, 16)
            split_hi(1, 1, 16)
            for n in range(2 * TILES):
                t, half = divmod(n, 2)
                act.wait_ge(h_tr, n + 1)
                act.activation(h_hi[:, 4 * half:4 * half + 4, t * P:(t + 1) * P],
                               ps[:, 5 + n % 3, :].rearrange("p (k n) -> p k n", k=4), ACT.Copy).then_inc(h_hi_rdy, 1)
            with act.Fori(0, 3) as it:
                for j in range(4):
                    after_slot(IN0, it, j)
            act.wait_ge(bank_empty, 25)
            for i, (lo, width) in enumerate(((0, QL), (QL, KVL))):
                for t in range(TILES):
                    if i or t:
                        act.wait_ge(z_ssq, i * TILES + t)
                    act.activation(junk_h[:, 0:width], z[:, t, lo:lo + width], ACT.Square,
                                   accum_out=ssq_z[:, i, t:t + 1]).then_inc(z_ssq, 1)
            for i, width in enumerate((QL, KVL)):
                act.wait_ge(z_ssq, 2 * TILES)
                act.activation(sd_z[:, i, 0:TILES], ssq_z[:, i, 0:TILES], ACT.Sqrt, scale=1.0 / width,
                               bias=eps_c[:, 0:1]).then_inc(z_sd, 1)

            def gates(base):
                with act.Fori(0, 2) as it:
                    for j in range(4):
                        b = 2 * (j % 2)
                        act.wait_ge(w_used, it * 4 + (base + j + 1))
                        if j >= 2:
                            act.wait_ge(g_st[j % 2], it * 32 + (base - G0) * 8 + 16)
                        act.activation(gate_s[:, j % 2, :].rearrange("p (n c) -> p n c", n=2), ps[:, b:b + 2, 0:HALF],
                                       ACT.Sigmoid).then_inc(g_sig, 1)
                        after_slot(base, it, j)
                    for u in range(2):
                        act.wait_ge(g_st[u], it * 32 + (base - G0) * 8 + 32)

            def job(j):
                kind, n = JOBS[j]
                bank = ps[:, 4 + j % 4, :]
                who = job_engine(kind, n)
                if who == "dve":
                    return
                act.wait_ge(job_full, j + 1)
                if kind == "qlat":
                    act.activation(ql_hi[:, :, n * P:(n + 1) * P], bank[:, 0:384].rearrange("p (k n) -> p k n", k=3),
                                   ACT.Copy).then_inc(job_act, 1)
                else:
                    copies = job_copies(kind, n, bank)
                    for i, (dst, src) in enumerate(copies):
                        ins = act.activation(dst, src, ACT.Copy)
                    ins.then_inc(job_act, 1)

            gates(G0)
            for j in range(JOBS1):
                job(j)
            gates(G1)
            act.wait_ge(g_st[0], 16 * 8)
            act.wait_ge(g_st[1], 16 * 8)
            for j in range(JOBS1, len(JOBS)):
                job(j)

            act.wait_ge(sink_rdy, 1)

            def exps(i):
                kind, a, b, c = BLOCKS[i]
                nk = n_keys(BLOCKS[i])
                lo = window(a)[1] if kind == "swa_p" else 0
                scale = MLA_SCALE if kind.startswith("mla") else SWA_SCALE
                col = slice(i % 4, i % 4 + 1)
                act.wait_ge(s_nm, i + 1)
                if i >= 3:
                    act.wait_ge(pt_full, i - 2)
                act.activation(probs[:, i % 3, lo:nk], ps[:, i % 3, lo:nk], ACT.Exp, scale=scale,
                               bias=nm_c[:, col], accum_out=sum_c[:, col]).then_inc(s_exp, 1)
                if kind.startswith("swa"):
                    sk = 4 if kind == "swa_s" else 2 * b + c
                    act.activation(es_c[:, col], sink_c[:, sk:sk + 1], ACT.Exp, bias=nm_c[:, col]).then_inc(s_es, 1)

            def pt_copy(k):
                kind, a, _, _ = BLOCKS[k]
                nk = n_keys(BLOCKS[k])
                full = -(-nk // P) * P if kind in ("swa_p", "mla_p") else P
                rows = CHUNK if kind == "swa_p" and nk % P else P
                act.wait_ge(pt_full, k + 1)
                if k >= 2:
                    act.wait_ge(pv_done, k - 1)
                bank = ps[:, 3 + k % 2, :]
                if kind == "swa_p" and rows == CHUNK:
                    if full > P:
                        act.activation(probs_T[:, k % 2, 0:full - P], bank[:, 0:full - P], ACT.Copy)
                    act.activation(probs_T[0:CHUNK, k % 2, full - P:full], bank[0:CHUNK, full - P:full],
                                   ACT.Copy).then_inc(pt_rdy, 1)
                elif kind in ("swa_p", "mla_p"):
                    act.activation(probs_T[:, k % 2, 0:full], bank[:, 0:full], ACT.Copy).then_inc(pt_rdy, 1)
                else:
                    act.activation(probs_T[:, k % 2, 0:P], bank[:, 0:P], ACT.Copy)
                    act.activation(probs_T[0:FRAMES, k % 2, P:2 * P], bank[0:FRAMES, P:2 * P],
                                   ACT.Copy).then_inc(pt_rdy, 1)

            def o_evac(k):
                g = GROUP[k]
                act.wait_ge(pv_done, k + 1)
                copies = o_copies(k, True)
                for dst, src in copies:
                    ins = act.activation(dst, src, ACT.Copy)
                ins.then_inc(o_hi, 1)

            for i in range(NB + 4):
                if i < NB:
                    exps(i)
                if 2 <= i < NB + 2:
                    pt_copy(i - 2)
                if 4 <= i and LAST_OF[i - 4]:
                    o_evac(i - 4)
            act.wait_ge(pv_done, NB + 1)
            act.activation(om_hi[:, :, SEQ:TOK], ps[:, 5 + NGROUPS % 2, :].rearrange("p (h n) -> p h n", h=4),
                           ACT.Copy).then_inc(o_hi, 1)

            with act.Fori(0, 2) as it:
                for j in range(4):
                    after_slot(BR0, it, j)
                    act.wait_ge(b_sum, it * 4 + (j + 1))
                    act.activation(m_hi[:, bass.ds(it * 4 + j, 1), :].rearrange("p a n -> p (a n)"),
                                   mix_s[:, j % 2, :], ACT.Copy).then_inc(b_hi, 1)
            for half in range(2):
                for j in range(4):
                    after_slot(WO0 + 4 * half, 0, j)
                for t in range(TILES):
                    act.wait_ge(bank_empty, 25 + 5 * half + t + 1)
                    if half or t:
                        act.wait_ge(m_ssq, 5 * half + t)
                    act.activation(junk_m[:, 0:512], x1[:, t, half * 512:(half + 1) * 512], ACT.Square,
                                   accum_out=ssq_a[:, half, t:t + 1]).then_inc(m_ssq, 1)
            for i in range(TILES + 2):
                if i < TILES:
                    act.wait_ge(m_tot, i + 1)
                    act.activation(rs_a[:, 1, i:i + 1], rs_a[:, 0, i:i + 1], ACT.Sqrt, scale=1.0 / D,
                                   bias=eps_c[:, 0:1]).then_inc(m_sd, 1)
                if 1 <= i <= TILES:
                    t = i - 1
                    act.wait_ge(x1_rdy, t + 1)
                    if t:
                        act.wait_ge(h2_ssq, t)
                    act.activation(junk_m[:], x1[:, t, :], ACT.Square, accum_out=ssq_h[:, t:t + 1]).then_inc(h2_ssq, 1)
                    act.wait_ge(h2_ssq, t + 1)
                    act.activation(sd_h[:, t:t + 1], ssq_h[:, t:t + 1], ACT.Sqrt, scale=1.0 / D,
                                   bias=eps_c[:, 0:1]).then_inc(h2_sd, 1)
                if i >= 2:
                    for half in range(2):
                        n = 2 * (i - 2) + half
                        act.wait_ge(h2_tr, n + 1)
                        act.activation(h2_hi[:, 4 * half:4 * half + 4, (i - 2) * P:(i - 1) * P],
                                       ps[:, 5 + n % 3, :].rearrange("p (k n) -> p k n", k=4),
                                       ACT.Copy).then_inc(h2_hi_rdy, 1)
            act.wait_ge(x1_st, 16 * TILES)
            with act.Fori(0, 11) as it:
                for q in range(2):
                    after_slot(GU0, it, 2 * q)
                    act.activation(silu_s[:, q, :].rearrange("p (n c) -> p n c", n=2), ps[:, 4 * q:4 * q + 2, 0:HALF],
                                   ACT.Silu).then_inc(u_silu, 1)
                    after_slot(GU0, it, 2 * q + 1)
                    act.wait_ge(u_prod, it * 2 + (q + 1))
                    act.activation(gu_hi[:, bass.ds(it * 2 + q, 1), :].rearrange("p a n -> p (a n)"), gu_s[:, q, :],
                                   ACT.Copy).then_inc(u_hi, 1)
            for half in range(2):
                for j in range(KF // 2):
                    u = half * (KF // 2) + j
                    if u + 2 < KF:
                        act.wait_ge(w_used, DN0 + u + 1)
                        s2 = DN0 + u + 2
                        split_hi(s2, s2 % 4, 16 * (s2 // 4 + 1))
                for t in range(TILES):
                    act.wait_ge(bank_empty, 45 + 5 * half + t + 1)
                    if half or t:
                        act.wait_ge(f_ssq, 5 * half + t)
                    act.activation(junk_f[:, 0:512], f_t[:, t, half * 512:(half + 1) * 512], ACT.Square,
                                   accum_out=ssq_z[:, half, t:t + 1]).then_inc(f_ssq, 1)
            for t in range(TILES):
                act.wait_ge(f_tot, t + 1)
                act.activation(sd_z[:, 1, t:t + 1], sd_z[:, 0, t:t + 1], ACT.Sqrt, scale=1.0 / D,
                               bias=eps_c[:, 0:1]).then_inc(f_sd, 1)

        @block.tensor
        def _(pe):
            def mm3(out, left, right, first, last):
                pe.matmul(out, left[1], right[0], start=first, stop=False)
                pe.matmul(out, left[0], right[1], start=False, stop=False)
                return pe.matmul(out, left[0], right[0], start=False, stop=last)

            def wide(r, act_hi, act_lo, banks, k0, k1):
                for k in range(k0, k1):
                    for n, bank in enumerate(banks):
                        w = slice(k * P, (k + 1) * P)
                        rows = slice(n * HALF, (n + 1) * HALF)
                        ins = mm3(ps[:, bank, 0:HALF], (whi[:, r, w], wlo[:, r, w]),
                                  (act_hi[:, k - k0, rows], act_lo[:, k - k0, rows]), k == k0, k == k1 - 1)
                return ins

            def tall(s_wait, r, width, a_hi, a_lo, k0, k_last, bank_wait, mm_sem):
                pe.wait_ge(w_lo, s_wait)
                for kk in range(2):
                    k = k0 + kk
                    for t in range(TILES):
                        if k == 0:
                            bank_wait(t)
                        w = slice(kk * width, (kk + 1) * width)
                        rows = slice(t * P, (t + 1) * P)
                        ins = mm3(ps[:, t, 0:width], (a_hi[:, k, rows], a_lo[:, k, rows]),
                                  (whi[:, r, w], wlo[:, r, w]), k == 0, k == k_last)
                        if k == k_last and t < TILES - 1:
                            ins.then_inc(mm_sem, 1)
                ins.then_inc(w_used, 1)

            pe.wait_ge(const_rdy, 3)
            for n in range(2 * TILES):
                t, half = divmod(n, 2)
                pe.wait_ge(h_norm, t + 1)
                if n >= 3:
                    pe.wait_ge(bank_empty, n - 2)
                for k in range(4):
                    c = (4 * half + k) * P
                    ins = pe.transpose(ps[:, 5 + n % 3, k * P:(k + 1) * P], x_t[:, t, c:c + P], ident[:])
                ins.then_inc(h_tr, 1)
            pe.wait_ge(bank_empty, 2 * TILES)
            with pe.Fori(0, 3) as it:
                for j in range(4):
                    tall(it * 4 + (j + 1), j % 2, IN_CHUNK, h_hi, h_lo, 2 * j, KD - 1,
                         lambda t: pe.wait_ge(bank_empty, it * 5 + (2 * TILES - 5 + t + 1)), z_mm)

            def gates(base):
                with pe.Fori(0, 2) as it:
                    for j in range(4):
                        pe.wait_ge(w_lo, it * 4 + (base + j + 1))
                        b = 2 * (j % 2)
                        wide(j % 2, h_hi, h_lo, (b, b + 1), 0, KD).then_inc(w_used, 1)

            pe.wait_ge(bank_empty, 25)
            gates(G0)

            def job(j):
                kind, n = JOBS[j]
                bank = ps[:, 4 + j % 4, :]
                if j >= 4:
                    job_emptied(pe, j - 4)
                c = slice(n * P, (n + 1) * P)
                if kind == "qlat":
                    for i in range(3):
                        ins = pe.transpose(bank[:, i * P:(i + 1) * P], z[:, n, i * P:(i + 1) * P], ident[:])
                elif kind == "ckv":
                    for i, c0 in enumerate((C_KV, C_KV + P, C_KS)):
                        pe.transpose(bank[:, i * P:(i + 1) * P], z[:, n, c0:c0 + P], ident[:])
                    ins = pe.transpose(bank[0:32, 384:512], z[:, n, C_PE:C_QS], ident[:])
                elif kind == "qs":
                    for i in range(4):
                        c0 = C_QS + i * P
                        ins = pe.transpose(bank[:, i * P:(i + 1) * P], z[:, n, c0:c0 + P], ident[:])
                elif kind == "uq":
                    t, half = divmod(n, 2)
                    job_emptied(pe, job_index("qlat", t))
                    if n == 0:
                        pe.wait_ge(wuq_rdy, 1)
                        pe.wait_ge(z_st, 16 * 24)
                    rows = slice(t * P, (t + 1) * P)
                    cols = slice(384 * half, 384 * half + 384)
                    for k in range(3):
                        ins = mm3(bank[:, 0:384], (ql_hi[:, k, rows], ql_lo[:, k, rows]),
                                  (wuq_hi[:, k, cols], wuq_lo[:, k, cols]), k == 0, k == 2)
                elif kind == "q":
                    t, half = divmod(n, 2)
                    if n == 0:
                        pe.wait_ge(q_rdy, 1)
                    for i in range(4):
                        ins = pe.transpose(bank[0:QK, i * P:(i + 1) * P], q_t[:, t, 4 * half + i, :], ident[:])
                elif kind == "cache":
                    pe.wait_ge(cache_in, 16 * 4)
                    for i in range(2):
                        pe.transpose(bank[:, i * P:(i + 1) * P], c_ckv[:, n, i * P:(i + 1) * P], ident[:])
                    pe.transpose(bank[:, 256:384], c_k[:, n, :], ident[:])
                    ins = pe.transpose(bank[0:32, 384:512], c_kpe[:, n, :], ident[:])
                elif kind == "wuk":
                    pe.wait_ge(wukv_in, 16 * 4)
                    for i in range(2):
                        for ct in range(2):
                            ins = pe.transpose(bank[0:64, (2 * i + ct) * P:(2 * i + ct + 1) * P],
                                               w_uk[:, ct, 2 * n + i, :], ident[:])
                elif kind == "qabs":
                    ct, half = divmod(n, 2)
                    if n == 0:
                        for i in range(4):
                            job_emptied(pe, job_index("wuk", i))
                        job_emptied(pe, job_index("q", 8))
                        job_emptied(pe, job_index("q", 9))
                    for i in range(4):
                        h = 4 * half + i
                        ins = pe.matmul(bank[:, i * P:(i + 1) * P], wuk_T[:, h, ct * P:(ct + 1) * P],
                                        q_Ts[0:NOPE, :, h, :], start=True, stop=True)
                elif kind == "kt":
                    for ct in range(2):
                        ins = pe.matmul(bank[:, :], w_uk[:, ct, 2 * n:2 * n + 2, :], ckv_T[:, ct, 0:SEQ],
                                        start=(ct == 0), stop=(ct == 1))
                else:
                    for ct in range(2):
                        ins = pe.matmul(bank[:, :], ckv_T[:, ct, c], w_uv[:, ct, :, :],
                                        start=(ct == 0), stop=(ct == 1))
                ins.then_inc(job_full, 1)

            pe.wait_ge(z_rdy, 1)
            for j in range(JOBS1):
                job(j)
            gates(G1)
            for j in range(JOBS1, len(JOBS)):
                job(j)

            pe.wait_ge(g_sig, 16)
            for j in range(len(JOBS) - 4, len(JOBS)):
                job_emptied(pe, j)
            pe.wait_ge(kpe_rdy, 1)
            pe.wait_ge(tails_rdy, 4)
            pe.wait_ge(new_in, 32)
            pe.wait_ge(v_s_rdy, 1)

            def scores(i):
                kind, a, b, c = BLOCKS[i]
                out = ps[:, i % 3, :]
                if i >= 3:
                    pe.wait_ge(s_exp, i - 2)
                if kind == "swa_p":
                    base, lo, hi = window(a)
                    rows = slice(64 * b, 64 * b + 64)
                    ins = pe.matmul(out[:, lo:hi], qs_T[rows, a, 2 * c:2 * c + 2, :],
                                    ks_T[rows, base + lo:base + hi], start=True, stop=True)
                elif kind == "swa_s":
                    for g in range(2):
                        rows = slice(64 * g, 64 * g + 64)
                        ins = pe.matmul(out[rows, 0:KEYS], qs_Ts[rows, a, :, :],
                                        k_Ta[rows, a, :], start=True, stop=True)
                elif kind == "mla_s":
                    for ct in range(2):
                        pe.matmul(out[:, 0:KEYS], qabs[:, ct, a, :, :], ckv_Ta[:, ct, a, :], start=(ct == 0), stop=False)
                    ins = pe.matmul(out[:, 0:KEYS], q_Ts[64:96, a, :, :],
                                    kpe_Ta[64:96, a, :], start=False, stop=True)
                else:
                    h, nk = 2 * a + c, (b + 1) * P
                    pe.matmul(out[:, 0:nk], q_T[0:QK, h, b * P:(b + 1) * P], k_T[0:QK, h, 0:nk], start=True, stop=False)
                    ins = pe.matmul(out[:, b * P:nk], mask_q[:], mask_k[:], start=False, stop=True)
                ins.then_inc(s_full, 1)

            def turn(k):
                kind, a, _, _ = BLOCKS[k]
                nk = n_keys(BLOCKS[k])
                pe.wait_ge(s_norm, k + 1)
                if k >= 2:
                    pe.wait_ge(pt_rdy, k - 1)
                for i in range(-(-nk // P)):
                    n = min(P, nk - i * P)
                    ins = pe.transpose(ps[0:n, 3 + k % 2, i * P:(i + 1) * P], probs[:, k % 3, i * P:i * P + n], ident[:])
                ins.then_inc(pt_full, 1)

            def outputs(k):
                kind, a, b, c = BLOCKS[k]
                g = GROUP[k]
                bank = ps[:, 5 + g % 2, :]
                pt = probs_T[:, k % 2, :]
                pe.wait_ge(pt_rdy, k + 1)
                if FIRST_OF[k] and g >= 2:
                    pe.wait_ge(o_hi, g - 1)
                    pe.wait_ge(o_lo, lo_groups(g - 1))
                if kind == "swa_p":
                    base, lo, hi = window(a)
                    pieces = []
                    for i in range(-(-hi // P)):
                        p0, p1 = max(lo - i * P, 0), min(hi - i * P, P)
                        pieces.append((base // P + i, i, p0, p1))
                    for u in range(2):
                        for n, (kt, i, p0, p1) in enumerate(pieces):
                            ins = pe.matmul(bank[64 * u:64 * u + 64, (2 * b + c) * CHUNK:(2 * b + c + 1) * CHUNK],
                                            v_s[p0:p1, kt, 64 * b:64 * b + 64],
                                            pt[p0:p1, i * P + 64 * u:i * P + 64 * u + 64],
                                            start=(n == 0), stop=(n == len(pieces) - 1))
                elif kind == "swa_s":
                    o = bank.rearrange("p (j n) -> p j n", j=4)
                    for gg in range(2):
                        rows = slice(64 * gg, 64 * gg + 64)
                        to = o[rows, :, a * FRAMES:(a + 1) * FRAMES]
                        pe.matmul(to, c_v[:, a, rows], pt[:, rows], start=True, stop=False)
                        ins = pe.matmul(to, v_new[:, a, rows], pt[0:FRAMES, P + 64 * gg:P + 64 * gg + 64],
                                        start=False, stop=True)
                elif kind == "mla_s":
                    for ct in range(2):
                        cc = slice(ct * P, (ct + 1) * P)
                        pe.matmul(bank[:, cc], c_ckv[:, a, cc], pt[:, 0:P], start=True, stop=False)
                        ins = pe.matmul(bank[:, cc], ckv_new[:, a, cc], pt[0:FRAMES, P:2 * P], start=False, stop=True)
                else:
                    h = 2 * a + c
                    for i in range(b + 1):
                        ins = pe.matmul(bank[64 * c:64 * c + 64, b * P:(b + 1) * P], v_p[:, i, 64 * h:64 * h + 64],
                                        pt[:, i * P:(i + 1) * P], start=(i == 0), stop=(i == b))
                ins.then_inc(pv_done, 1)

            for i in range(NB + 3):
                if i < NB:
                    scores(i)
                if 2 <= i < NB + 2:
                    turn(i - 2)
                if i >= 3:
                    outputs(i - 3)
            pe.wait_ge(o_hi, NGROUPS - 1)
            pe.wait_ge(o_lo, lo_groups(NGROUPS - 1))
            for h in range(HEADS):
                for ct in range(2):
                    ins = pe.matmul(ps[64 * (h % 2):64 * (h % 2) + 64, 5 + NGROUPS % 2, (h // 2) * P:(h // 2 + 1) * P],
                                    w_uv[:, ct, h, :], olat[:, ct, h, :], start=(ct == 0), stop=(ct == 1))
            ins.then_inc(pv_done, 1)
            pe.wait_ge(o_hi, NGROUPS + 1)
            pe.wait_ge(o_lo, lo_groups(NGROUPS) + 1)

            with pe.Fori(0, 2) as it:
                for j in range(4):
                    pe.wait_ge(w_lo, it * 4 + (BR0 + j + 1))
                    b = 4 * (j % 2)
                    wide(j % 2, om_hi, om_lo, (b, b + 1), 0, 4)
                    wide(j % 2, os_hi, os_lo, (b + 2, b + 3), 4, 8).then_inc(w_used, 1)

            def wo_bank(t, half):
                pe.wait_ge(bank_empty, 25 + 5 * half - 5 + t + 1)

            for half in range(2):
                for j in range(4):
                    if half == 0:
                        if j == 0:
                            pe.wait_ge(b_prod, 16)
                        pe.wait_ge(b_lo, 2 * (j + 1))
                    tall(WO0 + 4 * half + j + 1, j % 2, 512, m_hi, m_lo, 2 * j, KD - 1,
                         lambda t, half=half: wo_bank(t, half), wo_mm)
            for n in range(2 * TILES):
                t, half = divmod(n, 2)
                pe.wait_ge(h2_norm, t + 1)
                if n >= 3:
                    pe.wait_ge(bank_empty, 35 + n - 2)
                for k in range(4):
                    c = (4 * half + k) * P
                    ins = pe.transpose(ps[:, 5 + n % 3, k * P:(k + 1) * P], h2n[:, t % 2, c:c + P], ident[:])
                ins.then_inc(h2_tr, 1)
            pe.wait_ge(bank_empty, 35 + 2 * TILES)
            with pe.Fori(0, 11) as it:
                for q in range(2):
                    for i in range(2):
                        u = 2 * q + i
                        pe.wait_ge(w_lo, it * 4 + (GU0 + u + 1))
                        wide(u % 2, h2_hi, h2_lo, (2 * u, 2 * u + 1), 0, KD).then_inc(w_used, 1)
            for half in range(2):
                for j in range(KF // 2):
                    u = half * (KF // 2) + j
                    if half == 0:
                        if j == 0:
                            pe.wait_ge(u_silu, KF)
                            pe.wait_ge(u_prod, KF)
                        pe.wait_ge(u_lo, 2 * (j + 1))
                    tall(DN0 + u + 1, u % 2, 512, gu_hi, gu_lo, 2 * j, KF - 1,
                         lambda t, half=half: pe.wait_ge(bank_empty, 45 + 5 * half - 5 + t + 1), f_mm)

        @block.vector
        def _(dve):
            def split_lo(s1, r):
                dve.wait_ge(w_hi, s1)
                dve.tensor_tensor(wlo[:, r % 2, :], raw[:, r, :], whi[:, r % 2, :].bitcast(F32),
                                  ALU.subtract).then_inc(w_lo, 1)

            def after_slot(base, it, j):
                split_lo(it * 4 + (base + j + 3), (base + j + 2) % 4)

            dve.wait_ge(gpre_in, 16)
            for t in range(TILES):
                dve.wait_ge(h_sd, t + 1)
                dve.reciprocal(r_h[:, t:t + 1], sd_h[:, t:t + 1]).then_inc(h_rs, 1)
                dve.wait_ge(h_rs, t + 1)
                dve.scalar_tensor_tensor(out=x_t[:, t, :], in0=x_t[:, t, :], scalar=r_h[:, t:t + 1], in1=gpre_b[:],
                                         op0=ALU.mult, op1=ALU.mult).then_inc(h_norm, 1)
            split_lo(1, 0)
            split_lo(2, 1)
            for n in range(2 * TILES):
                t, half = divmod(n, 2)
                to = slice(4 * half, 4 * half + 4), slice(t * P, (t + 1) * P)
                dve.wait_ge(h_hi_rdy, n + 1)
                dve.tensor_tensor(h_lo[:, to[0], to[1]], ps[:, 5 + n % 3, :].rearrange("p (k n) -> p k n", k=4),
                                  h_hi[:, to[0], to[1]].bitcast(F32), ALU.subtract).then_inc(bank_empty, 1)
            with dve.Fori(0, 3) as it:
                for j in range(4):
                    if j == 3:
                        for t in range(TILES):
                            if t < TILES - 1:
                                dve.wait_ge(z_mm, it * 4 + (t + 1))
                            else:
                                dve.wait_ge(w_used, it * 4 + 4)
                            dve.tensor_copy(z[:, t, bass.ds(it * IN_CHUNK, IN_CHUNK)],
                                            ps[:, t, 0:IN_CHUNK]).then_inc(bank_empty, 1)
                    after_slot(IN0, it, j)
            for i in range(2):
                dve.wait_ge(z_sd, i + 1)
                dve.reciprocal(r_z[:, i, 0:TILES], sd_z[:, i, 0:TILES]).then_inc(z_rs, 1)

            def gates(base):
                with dve.Fori(0, 2) as it:
                    for j in range(4):
                        after_slot(base, it, j)

            def job(j):
                kind, n = JOBS[j]
                bank = ps[:, 4 + j % 4, :]
                who = job_engine(kind, n)
                if who == "act":
                    return
                if kind == "qlat":
                    dve.wait_ge(job_act, JOB_COUNTS[j][0])
                    c = slice(n * P, (n + 1) * P)
                    dve.tensor_tensor(ql_lo[:, :, c], bank[:, 0:384].rearrange("p (k n) -> p k n", k=3),
                                      ql_hi[:, :, c].bitcast(F32), ALU.subtract).then_inc(job_dve, 1)
                    return
                dve.wait_ge(job_full, j + 1)
                for dst, src in job_copies(kind, n, bank):
                    ins = dve.tensor_copy(dst, src)
                ins.then_inc(job_dve, 1)

            gates(G0)
            for j in range(JOBS1):
                job(j)
            gates(G1)
            dve.wait_ge(w_used, BR0)
            dve.tensor_copy(k_T[64:96, :, :], kpe_T[64:96, 0:SEQ].unsqueeze(1).to_broadcast([32, HEADS, SEQ])).then_inc(kpe_rdy, 1)
            for j in range(JOBS1, len(JOBS)):
                job(j)

            dve.wait_ge(sink_rdy, 1)
            dve.memset(probs[:], 0.0).then_inc(kpe_rdy, 1)

            def row_max(i):
                kind, a, b, c = BLOCKS[i]
                nk = n_keys(BLOCKS[i])
                lo = window(a)[1] if kind == "swa_p" else 0
                col = slice(i % 4, i % 4 + 1)
                dve.wait_ge(s_full, i + 1)
                dve.tensor_reduce(mx_c[:, col], ps[:, i % 3, lo:nk], AX_X, ALU.max).then_inc(s_max, 1)
                dve.wait_ge(s_max, i + 1)
                if kind.startswith("swa"):
                    sk = 4 if kind == "swa_s" else 2 * b + c
                    dve.tensor_scalar(nm_c[:, col], mx_c[:, col], -SWA_SCALE, nsink_c[:, sk:sk + 1], ALU.mult,
                                      ALU.min).then_inc(s_nm, 1)
                else:
                    dve.tensor_scalar(nm_c[:, col], mx_c[:, col], -MLA_SCALE, None, ALU.mult).then_inc(s_nm, 1)

            n_es = [0]
            es_at = []
            for kind, _, _, _ in BLOCKS:
                n_es[0] += kind.startswith("swa")
                es_at.append(n_es[0])

            def normalise(k):
                kind, a, _, _ = BLOCKS[k]
                nk = n_keys(BLOCKS[k])
                lo = window(a)[1] if kind == "swa_p" else 0
                col = slice(k % 4, k % 4 + 1)
                dve.wait_ge(s_exp, k + 1)
                total = sum_c
                if kind.startswith("swa"):
                    dve.wait_ge(s_es, es_at[k])
                    dve.tensor_tensor(den_c[:, col], sum_c[:, col], es_c[:, col], ALU.add).then_inc(s_den, 1)
                    dve.wait_ge(s_den, es_at[k])
                    total = den_c
                dve.reciprocal(inv_c[:, col], total[:, col]).then_inc(s_inv, 1)
                dve.wait_ge(s_inv, k + 1)
                dve.tensor_scalar(probs[:, k % 3, lo:nk], probs[:, k % 3, lo:nk], inv_c[:, col], None,
                                  ALU.mult).then_inc(s_norm, 1)

            def o_evac(k):
                g = GROUP[k]
                if GROUP_KIND[g] == "mla_s":
                    return
                dve.wait_ge(o_hi, g + 1)
                for (dst, src), (hi_part, _) in zip(o_copies(k, False), o_copies(k, True)):
                    ins = dve.tensor_tensor(dst, src, hi_part.bitcast(F32), ALU.subtract)
                ins.then_inc(o_lo, 1)

            for i in range(NB + 4):
                if i < NB:
                    row_max(i)
                if 1 <= i < NB + 1:
                    normalise(i - 1)
                if 4 <= i and LAST_OF[i - 4]:
                    o_evac(i - 4)
            dve.wait_ge(o_hi, NGROUPS + 1)
            dve.tensor_tensor(om_lo[:, :, SEQ:TOK], ps[:, 5 + NGROUPS % 2, :].rearrange("p (h n) -> p h n", h=4),
                              om_hi[:, :, SEQ:TOK].bitcast(F32), ALU.subtract).then_inc(o_lo, 1)

            with dve.Fori(0, 2) as it:
                for j in range(4):
                    m = it * 4 + j
                    dve.wait_ge(w_used, it * 4 + (BR0 + j + 1))
                    dve.wait_ge(g_ld[j % 2], it * 32 + 16 * (j // 2 + 1))
                    for b, to in enumerate((mix_a, mix_b)):
                        bank = 4 * (j % 2) + 2 * b
                        dve.tensor_tensor(to[:].rearrange("p (n c) -> p n c", n=2), ps[:, bank:bank + 2, 0:HALF],
                                          gate_r[:, j % 2, b, :].rearrange("p (n c) -> p n c", n=2),
                                          ALU.mult).then_inc(b_prod, 1)
                    dve.wait_ge(b_prod, it * 8 + 2 * (j + 1))
                    dve.tensor_tensor(mix_s[:, j % 2, :], mix_a[:], mix_b[:], ALU.add).then_inc(b_sum, 1)
                    after_slot(BR0, it, j)
                    dve.wait_ge(b_hi, it * 4 + (j + 1))
                    dve.tensor_tensor(m_lo[:, bass.ds(m, 1), :].rearrange("p a n -> p (a n)"), mix_s[:, j % 2, :],
                                      m_hi[:, bass.ds(m, 1), :].rearrange("p a n -> p (a n)").bitcast(F32),
                                      ALU.subtract).then_inc(b_lo, 1)
            for half in range(2):
                for j in range(4):
                    if j == 3:
                        for t in range(TILES):
                            if t < TILES - 1:
                                dve.wait_ge(wo_mm, 4 * half + t + 1)
                            else:
                                dve.wait_ge(w_used, WO0 + 4 * half + 4)
                            dve.tensor_copy(x1[:, t, half * 512:(half + 1) * 512], ps[:, t, :]).then_inc(bank_empty, 1)
                    after_slot(WO0 + 4 * half, 0, j)
            dve.wait_ge(wo_in, 16 * (TILES + 2))
            for i in range(TILES + 2):
                if i < TILES:
                    c = slice(i, i + 1)
                    dve.wait_ge(m_ssq, TILES + i + 1)
                    dve.tensor_tensor(rs_a[:, 0, c], ssq_a[:, 0, c], ssq_a[:, 1, c], ALU.add).then_inc(m_tot, 1)
                    dve.wait_ge(m_sd, i + 1)
                    dve.reciprocal(rs_a[:, 2, c], rs_a[:, 1, c]).then_inc(m_rs, 1)
                    dve.wait_ge(m_rs, i + 1)
                    dve.scalar_tensor_tensor(out=x1[:, i, :], in0=x1[:, i, :], scalar=rs_a[:, 2, c], in1=gpm_b[:],
                                             op0=ALU.mult, op1=ALU.mult).then_inc(m_sc, 1)
                    dve.wait_ge(m_sc, i + 1)
                    dve.tensor_tensor(x1[:, i, :], x1[:, i, :], x_r[:, i, :], ALU.add).then_inc(x1_rdy, 1)
                if 1 <= i <= TILES:
                    t = i - 1
                    c = slice(t, t + 1)
                    dve.wait_ge(h2_sd, t + 1)
                    dve.reciprocal(r_h[:, c], sd_h[:, c]).then_inc(h2_rs, 1)
                    dve.wait_ge(h2_rs, t + 1)
                    if t >= 2:
                        dve.wait_ge(h2_tr, 2 * (t - 1))
                    dve.scalar_tensor_tensor(out=h2n[:, t % 2, :], in0=x1[:, t, :], scalar=r_h[:, c], in1=gpf_b[:],
                                             op0=ALU.mult, op1=ALU.mult).then_inc(h2_norm, 1)
                if i >= 2:
                    for half in range(2):
                        n = 2 * (i - 2) + half
                        to = slice(4 * half, 4 * half + 4), slice((i - 2) * P, (i - 1) * P)
                        dve.wait_ge(h2_hi_rdy, n + 1)
                        dve.tensor_tensor(h2_lo[:, to[0], to[1]], ps[:, 5 + n % 3, :].rearrange("p (k n) -> p k n", k=4),
                                          h2_hi[:, to[0], to[1]].bitcast(F32), ALU.subtract).then_inc(bank_empty, 1)
            dve.wait_ge(x1_st, 16 * TILES)
            with dve.Fori(0, 11) as it:
                for q in range(2):
                    after_slot(GU0, it, 2 * q)
                    dve.wait_ge(w_used, it * 4 + (GU0 + 2 * q + 2))
                    dve.wait_ge(u_silu, it * 2 + (q + 1))
                    dve.tensor_tensor(gu_s[:, q, :].rearrange("p (n c) -> p n c", n=2), ps[:, 4 * q + 2:4 * q + 4, 0:HALF],
                                      silu_s[:, q, :].rearrange("p (n c) -> p n c", n=2), ALU.mult).then_inc(u_prod, 1)
                    after_slot(GU0, it, 2 * q + 1)
                    dve.wait_ge(u_hi, it * 2 + (q + 1))
                    f = bass.ds(it * 2 + q, 1)
                    dve.tensor_tensor(gu_lo[:, f, :].rearrange("p a n -> p (a n)"), gu_s[:, q, :],
                                      gu_hi[:, f, :].rearrange("p a n -> p (a n)").bitcast(F32),
                                      ALU.subtract).then_inc(u_lo, 1)
            for half in range(2):
                for j in range(KF // 2):
                    u = half * (KF // 2) + j
                    if j == KF // 2 - 1:
                        for t in range(TILES):
                            if t < TILES - 1:
                                dve.wait_ge(f_mm, 4 * half + t + 1)
                            else:
                                dve.wait_ge(w_used, DN0 + u + 1)
                            dve.tensor_copy(f_t[:, t, half * 512:(half + 1) * 512], ps[:, t, :]).then_inc(bank_empty, 1)
                    if u + 2 < KF:
                        split_lo(DN0 + u + 3, (DN0 + u + 2) % 4)
            dve.wait_ge(gpo_in, 16)
            dve.wait_ge(x1_in, 16)
            for t in range(TILES):
                c = slice(t, t + 1)
                dve.wait_ge(f_ssq, TILES + t + 1)
                dve.tensor_tensor(sd_z[:, 0, c], ssq_z[:, 0, c], ssq_z[:, 1, c], ALU.add).then_inc(f_tot, 1)
            for t in range(TILES):
                c = slice(t, t + 1)
                dve.wait_ge(f_sd, t + 1)
                dve.reciprocal(r_z[:, 0, c], sd_z[:, 1, c]).then_inc(f_rs, 1)
                dve.wait_ge(f_rs, t + 1)
                dve.scalar_tensor_tensor(out=f_t[:, t, :], in0=f_t[:, t, :], scalar=r_z[:, 0, c], in1=gpo_b[:],
                                         op0=ALU.mult, op1=ALU.mult).then_inc(f_sc, 1)
                dve.wait_ge(f_sc, t + 1)
                dve.tensor_tensor(f_t[:, t, :], f_t[:, t, :], x1_r[:, t, :], ALU.add).then_inc(y_rdy, 1)


_INS = ["x_prompt", "x_sample", "cache_mla_ckv", "cache_mla_kpe", "cache_swa_k", "cache_swa_v", "g_pre_mix", "w_in",
        "g_q", "w_uq", "g_kv", "w_ukv", "swa_sinks", "w_branch", "w_out", "g_post_mix", "g_pre_ffn", "w_gate_up",
        "w_down", "g_post_ffn"]
_OUTS = [(1, SEQ, D), (STREAMS, FRAMES, D), (1, 1, SEQ, KVL), (1, 1, SEQ, ROPE), (1, 1, PAST, KV_HEADS, HD),
         (1, 1, PAST, KV_HEADS, HD), (1, STREAMS, FRAMES, KVL), (1, STREAMS, FRAMES, ROPE),
         (1, STREAMS, PAST, KV_HEADS, HD), (1, STREAMS, PAST, KV_HEADS, HD)]


def kernel(**inputs):
    import concourse.bacc as _bacc
    from concourse.bass_utils import run_bass_kernel_spmd as _run

    nc = _bacc.Bacc("TRN2", target_bir_lowering=False, num_devices=1)
    arrays, args = {}, []
    for name in _INS:
        a = np.ascontiguousarray(inputs[name])
        arrays[f"in_{name}"] = a
        args.append(nc.dram_tensor(f"in_{name}", a.shape, mybir.dt.from_np(a.dtype), kind="ExternalInput").ap())
    for i, shape in enumerate(_OUTS):
        args.append(nc.dram_tensor(f"out_{i}", shape, F32, kind="ExternalOutput").ap())
    build_layer(nc, *args)
    r = _run(nc, [arrays], core_ids=[0])
    return tuple(r.results[0][f"out_{i}"] for i in range(len(_OUTS)))
```

```python
from contextlib import ExitStack

import numpy as np

import concourse.bass as bass
from concourse import mybir

F32 = mybir.dt.float32
F32R = mybir.dt.float32r
BF16 = mybir.dt.bfloat16
ALU = mybir.AluOpType
ACT = mybir.ActivationFunctionType
AX_X = mybir.AxisListType.X

P = 128
D = 1024
SEQ = 512
STREAMS = 8
FRAMES = 16
PAST = 128
CHUNK = 64
TOK = SEQ + STREAMS * FRAMES
TILES = TOK // P
HALF = TOK // 2
KD = D // P
HEADS = 8
NOPE, ROPE, VDIM = 64, 32, 64
QK = NOPE + ROPE
QL, KVL = 384, 256
HD = 64
KV_HEADS = 2
MIX_COLS = 1440
IN_CHUNK = 480
DFF = 2816
KF = DFF // P
EPS = 1e-6
MLA_SCALE = QK ** -0.5
SWA_SCALE = HD ** -0.5
KEYS = PAST + FRAMES

C_KV, C_PE, C_QS, C_KS, C_VS = QL, QL + KVL, QL + KVL + ROPE, 1184, 1312

IN0, G0, G1, BR0, WO0, GU0, DN0 = 0, 12, 20, 28, 36, 44, 88
SLOTS = DN0 + KF

JOBS = (
    [(kind, t) for t in range(TILES) for kind in ("qlat", "ckv", "qs")]
    + [("uq", n) for n in range(2 * TILES)]
    + [("kt", n) for n in range(4)] + [("q", n) for n in range(2 * TILES)] + [("cache", b) for b in range(STREAMS)]
    + [("wuk", n) for n in range(4)] + [("v", 0), ("v", 1)] + [("qabs", n) for n in range(4)] + [("v", 2), ("v", 3)]
)
JOBS1 = 5 * TILES


def job_bank(j):
    return 4 + j % 4 if j < JOBS1 else (j - JOBS1) % 4


def job_engine(kind, n):
    if kind == "qlat":
        return "both"
    if kind == "ckv":
        return "dve"
    if kind == "qs":
        return "act"
    return "act" if n % 2 else "dve"


def job_counts():
    act = dve = 0
    out = []
    for kind, n in JOBS:
        who = job_engine(kind, n)
        act += who != "dve"
        dve += who != "act"
        out.append((act, dve))
    return out


JOB_COUNTS = job_counts()

LATENT = {(i, n): ("mla_p", i, n // 2, n % 2) for i in range(SEQ // P) for n in range(HEADS)}
BLOCKS = [("swa_p", c, g, jp) for c in range(SEQ // CHUNK) for g in range(KV_HEADS) for jp in range(2)]
for n in range(HEADS):
    BLOCKS += [("mla_s", n, 0, 0), LATENT[3, n]]
for n in range(HEADS):
    BLOCKS.append(LATENT[2, n])
    if 2 <= n < 2 + STREAMS // 2:
        BLOCKS += [("swa_s", 2 * n - 4, 0, 0), ("swa_s", 2 * n - 3, 0, 0)]
BLOCKS += [LATENT[i, n] for i in (1, 0) for n in range(HEADS)]
NB = len(BLOCKS)


def group_key(block):
    return (block[0], 0 if block[0] == "swa_s" else block[1])


KEYS_IN_ORDER = [group_key(b) for b in BLOCKS]
FIRST_OF = [KEYS_IN_ORDER.index(KEYS_IN_ORDER[n]) == n for n in range(NB)]
LAST_OF = [KEYS_IN_ORDER[n] not in KEYS_IN_ORDER[n + 1:] for n in range(NB)]
ENDED = [KEYS_IN_ORDER[n] for n in range(NB) if LAST_OF[n]]
GROUP = [ENDED.index(key) for key in KEYS_IN_ORDER]
NGROUPS = len(ENDED)
GROUP_KIND = {g: key[0] for g, key in enumerate(ENDED)}
VALUE_BANK = 6
F_BANK = (0, 5)
SINK_AT = (192, 448)
OUT_BANK = {("mla_p", 3): 6, ("mla_p", 2): 7, ("mla_p", 1): 6, ("mla_p", 0): 7, ("swa_s", 0): 6}
NA = 4 * (SEQ // CHUNK)


def score_bank(i):
    return 4 + i % 2 if i < NA else i % 4


def score_place(i):
    kind, c, _, _ = BLOCKS[i]
    nk = n_keys(BLOCKS[i])
    if kind == "swa_p":
        lo = window(c)[1]
        end = SINK_AT[i % 4 // 2]
        return end - (nk - lo), end + 1, lo
    return 0, nk + (kind == "swa_s"), 0


def turn_bank(i):
    return 6 if i < NA else 4 + i % 2


def out_bank(g):
    return 7 if g < SEQ // CHUNK else OUT_BANK.get(ENDED[g], 7)


def last_in_bank(g):
    first = GROUP.index(g)
    found = [h for h in range(g) if out_bank(h) == out_bank(g) and max(n for n in range(NB) if GROUP[n] == h) < first]
    return found[-1] if found else None


def lo_groups(upto):
    return sum(GROUP_KIND[g] != "mla_s" for g in range(upto))


def window(c):
    base = max(0, (c // 2 - 1)) * P
    return base, max(0, c - 2) * CHUNK - base, (c + 1) * CHUNK - base


def n_keys(block):
    kind, a, b, _ = block
    if kind == "swa_p":
        return window(a)[2]
    if kind == "mla_p":
        return (a + 1) * P
    return KEYS


def rope_tables():
    half = HD // 2
    inv = np.float32(10000.0) ** (-np.arange(half, dtype=np.float32) / np.float32(half))
    pos = np.concatenate([np.arange(SEQ), PAST + np.arange(STREAMS * FRAMES) % FRAMES]).astype(np.float32)
    ang = (pos[:, None] * inv[None, :].astype(np.float32)).astype(np.float32)
    shape = lambda a: np.ascontiguousarray(
        a.astype(np.float32).reshape(TILES, P, half).transpose(1, 0, 2).reshape(P, TILES * half))
    return shape(np.cos(ang)), shape(np.sin(ang))


def build_layer(nc, x_prompt, x_sample, cache_mla_ckv, cache_mla_kpe, cache_swa_k, cache_swa_v,
                g_pre_mix, w_in, g_q, w_uq, g_kv, w_ukv, swa_sinks, w_branch, w_out,
                g_post_mix, g_pre_ffn, w_gate_up, w_down, g_post_ffn,
                y_prompt, y_sample, p_ckv, p_kpe, p_k, p_v, s_ckv, s_kpe, s_k, s_v):
    cos_np, sin_np = rope_tables()
    cos_dram = nc.inline_tensor(cos_np, "rope_cos").ap()
    sin_dram = nc.inline_tensor(sin_np, "rope_sin").ap()
    gates_dram = nc.dram_tensor("gates_scratch", (16, P, TOK), F32, kind="Internal").ap()
    x1_dram = nc.dram_tensor("x1_scratch", (P, TILES, D), F32, kind="Internal").ap()

    win_v = w_in[0].rearrange("(k p) n -> p k n", p=P)
    wbr_v = w_branch[0].rearrange("b (t p) n -> p (b t) n", p=P)
    wout_v = w_out[0].rearrange("(k p) n -> p k n", p=P)
    wgu_v = w_gate_up[0].rearrange("(k p) n -> p k n", p=P)
    wdn_v = w_down[0].rearrange("(k p) n -> p k n", p=P)

    def x_rows(t):
        return x_prompt[0, t * P:(t + 1) * P, :] if t < 4 else x_sample.rearrange("b t d -> (b t) d")

    def y_rows(t):
        return y_prompt[0, t * P:(t + 1) * P, :] if t < 4 else y_sample.rearrange("b t d -> (b t) d")

    SB0 = 16512

    def at(name, shape, word, dt=F32):
        return nc.alloc_sbuf_tensor_at(name, shape, dt, offset=SB0 + 4 * word)

    raw = at("raw", [P, 4, 1024], 0)
    whi = at("whi", [P, 2, 1024], 4096, F32R)
    wlo = at("wlo", [P, 2, 1024], 6144, F32R)
    ident = at("ident", [P, P], 8192)
    cos_t = at("cos_t", [P, TILES, 32], 8320)
    sin_t = at("sin_t", [P, TILES, 32], 8480)
    gq_b = at("gq_b", [P, QL], 8640)
    gkv_b = at("gkv_b", [P, KVL], 9024)
    ssq_h = at("ssq_h", [P, 8], 9280)
    sd_h = at("sd_h", [P, 8], 9288)
    r_h = at("r_h", [P, 8], 9296)
    ssq_z = at("ssq_z", [P, 2, 8], 9304)
    sd_z = at("sd_z", [P, 2, 8], 9320)
    r_z = at("r_z", [P, 2, 8], 9336)
    nm_c = at("nm_c", [P, 8], 9360)
    sum_c = at("sum_c", [P, 8], 9368)
    inv_c = at("inv_c", [P, 8], 9376)


    sink_b = at("sink_b", [P, HEADS], 9400)
    one_c = at("one_c", [1, 8], 9408)


    eps_c = at("eps_c", [P, 8], 9424)
    mask_q = at("mask_q", [1, P], 9432, BF16)
    mask_k = at("mask_k", [1, P], 9496, BF16)
    ssq_a = at("ssq_a", [P, 2, 8], 9560)
    rs_a = at("rs_a", [P, 3, 8], 9576)

    def area(name, shape, word, dt=F32):
        return at(name, shape, 9600 + word, dt)

    h_hi = area("h_hi", [P, KD, TOK], 0, F32R)
    h_lo = area("h_lo", [P, KD, TOK], 5120, F32R)
    x_t = area("x_t", [P, TILES, D], 10240)
    junk_h = area("junk_h", [P, D], 27680)
    gpre_b = area("gpre_b", [P, D], 42400)
    in_hi = area("in_hi", [P, 2, 1024], 28704, F32R)
    in_lo = area("in_lo", [P, 2, 1024], 30752, F32R)
    ql_hi = area("ql_hi", [P, 3, TOK], 10240, F32R)
    ql_lo = area("ql_lo", [P, 3, TOK], 12160, F32R)
    wuq_hi = area("wuq_hi", [P, 3, 768], 15360, F32R)
    wuq_lo = area("wuq_lo", [P, 3, 768], 17664, F32R)
    wuq_raw = area("wuq_raw", [P, 3, 768], 37536)
    z = area("z", [P, TILES, MIX_COLS], 20480)
    rope_a = area("rope_a", [P, TILES, 10, 32], 35488)
    rope_b = area("rope_b", [P, TILES, 10, 32], 37088)
    rope_c = area("rope_c", [P, TILES, 10, 32], 38688)
    rope_d = area("rope_d", [P, TILES, 10, 32], 40288)
    gate_s = area("gate_s", [P, 2, TOK], 14080)
    gate_s1 = area("gate_s1", [P, 2, TOK], 35488)
    q_t = area("q_t", [P, TILES, HEADS, QK], 20480)
    qro_a = area("qro_a", [P, TILES, HEADS, 16], 36768)
    qro_b = area("qro_b", [P, TILES, HEADS, 16], 37408)
    qro_c = area("qro_c", [P, TILES, HEADS, 16], 38048)
    qro_d = area("qro_d", [P, TILES, HEADS, 16], 38688)
    qs_T = area("qs_T", [P, SEQ // CHUNK, 4, CHUNK], 27680)
    qs_Ts = area("qs_Ts", [P, STREAMS, 4, FRAMES], 29728)
    ks_T = area("ks_T", [P, TOK], 30240)
    v_s = area("v_s", [P, TILES, P], 30880)
    ckv_T = area("ckv_T", [P, 2, TOK], 31520)
    kpe_T = area("kpe_T", [P, TOK], 32800)
    sink_s = area("sink_s", [1, HEADS, FRAMES], 33312)
    w_uk = area("w_uk", [P, 2, HEADS, NOPE], 33440)
    w_uv = area("w_uv", [P, 2, HEADS, VDIM], 34464)
    wuk_T = area("wuk_T", [64, HEADS, KVL], 35488)
    olat = area("olat", [P, 2, HEADS, P], 35488)
    ckv_Ta = area("ckv_Ta", [P, 2, STREAMS, KEYS], 37536)
    kpe_Ta = area("kpe_Ta", [P, STREAMS, KEYS], 39840)
    k_Ta = area("k_Ta", [P, STREAMS, KEYS], 40992)
    c_kpe = area("c_kpe", [P, STREAMS, ROPE], 42144)
    c_v = area("c_v", [P, STREAMS, P], 42400)
    c_ckv = area("c_ckv", [P, STREAMS, KVL], 15360)
    ckv_new = area("ckv_new", [FRAMES, STREAMS, KVL], 17408)
    c_k = area("c_k", [P, STREAMS, P], 19456)
    q_T = area("q_T", [P, HEADS, SEQ], 0)
    q_Ts = area("q_Ts", [P, STREAMS, HEADS, FRAMES], 4096)
    k_T = area("k_T", [P, HEADS, SEQ], 5120)
    v_new = area("v_new", [FRAMES, STREAMS, P], 9216)
    v_p = area("v_p", [P, 4, SEQ], 20480)
    qabs = area("qabs", [P, 2, STREAMS, HEADS, FRAMES], 22528)
    probs = area("probs", [P, 4, 512], 24608)
    probs_T = area("probs_T", [P, 2, 512], 26656)
    os_hi = area("os_hi", [P, 4, TOK], 10240, F32R)
    os_lo = area("os_lo", [P, 4, TOK], 12800, F32R)
    om_hi = area("om_hi", [P, 4, TOK], 15360, F32R)
    om_lo = area("om_lo", [P, 4, TOK], 17920, F32R)
    gate_r = area("gate_r", [P, 2, 2, TOK], 27680)
    mix_a = area("mix_a", [P, TOK], 30240)
    mix_b = area("mix_b", [P, TOK], 30880)
    mix_s = area("mix_s", [P, 2, TOK], 31520)
    m_hi = area("m_hi", [P, KD, TOK], 0, F32R)
    m_lo = area("m_lo", [P, KD, TOK], 5120, F32R)
    x1 = area("x1", [P, TILES, D], 10240)
    x_r = area("x_r", [P, TILES, D], 15360)
    gpm_b = area("gpm_b", [P, D], 20480)
    gpf_b = area("gpf_b", [P, D], 21504)
    wo_hi = area("wo_hi", [P, 4, 1024], 22528, F32R)
    wo_lo = area("wo_lo", [P, 4, 1024], 26624, F32R)
    junk_m = area("junk_m", [P, D], 30720)
    h2_hi = area("h2_hi", [P, KD, TOK], 33296, F32R)
    h2_lo = area("h2_lo", [P, KD, TOK], 38416, F32R)
    gu_hi = area("gu_hi", [P, KF, TOK], 0, F32R)
    gu_lo = area("gu_lo", [P, KF, TOK], KF * TOK, F32R)
    silu_s = area("silu_s", [P, 2, TOK], 28160)
    gu_s = area("gu_s", [P, 2, TOK], 29440)
    gpo_b = area("gpo_b", [P, D], 30720)
    dn_hi = area("dn_hi", [P, 1, 1024], 28160, F32R)
    dn_lo = area("dn_lo", [P, 1, 1024], 29184, F32R)
    junk_f = area("junk_f", [P, D], 31744)
    f_t = area("f_t", [P, TILES, D], 33296)
    x1_r = area("x1_r", [P, TILES, D], 38416)

    with ExitStack() as ctx:
        ps = ctx.enter_context(nc.psum_tensor("ps", [P, 8, 512], F32))

        def sem(name):
            return ctx.enter_context(nc.semaphore(name))

        x_in = [sem(f"x_in{t}") for t in range(TILES)]
        gpre_in, tab_in, wuq_in, wukv_in, sink_in = (sem(n) for n in ("gpre_in", "tab_in", "wuq_in", "wukv_in", "sink_in"))
        w_raw = [sem(f"w_raw{r}") for r in range(4)]
        w_hi, w_lo, w_used = sem("w_hi"), sem("w_lo"), sem("w_used")
        eps_rdy, pad_rdy, const_rdy, sink_rdy = sem("eps_rdy"), sem("pad_rdy"), sem("const_rdy"), sem("sink_rdy")
        h_ssq, h_sd, h_rs, h_norm, h_tr, h_hi_rdy, h_lo_rdy = (sem(n) for n in ("h_ssq", "h_sd", "h_rs", "h_norm", "h_tr", "h_hi_rdy", "h_lo_rdy"))
        bank_empty = sem("bank_empty")
        z_mm = sem("z_mm")
        z_ssq, z_sd, z_rs, z_norm = sem("z_ssq"), sem("z_sd"), sem("z_rs"), sem("z_norm")
        pool_step, z_st, v_s_rdy = sem("pool_step"), sem("z_st"), sem("v_s_rdy")
        wuq_rdy, tails_rdy = sem("wuq_rdy"), sem("tails_rdy")
        g_out, g_sig = sem("g_out"), sem("g_sig")
        g_st = [sem("g_st0"), sem("g_st1")]
        job_full, job_act, job_dve = sem("job_full"), sem("job_act"), sem("job_dve")
        kpe_rdy = sem("kpe_rdy")
        cache_in, new_in = sem("cache_in"), sem("new_in")
        probs_rdy, s_full, s_nm, s_exp, s_inv, s_norm = (
            sem(n) for n in ("probs_rdy", "s_full", "s_nm", "s_exp", "s_inv", "s_norm"))
        pt_full, pt_rdy, pv_done, o_hi, o_lo = (
            sem(n) for n in ("pt_full", "pt_rdy", "pv_done", "o_hi", "o_lo"))
        g_ld = [sem("g_ld0"), sem("g_ld1")]
        b_prod, b_sum, b_hi, b_lo = sem("b_prod"), sem("b_sum"), sem("b_hi"), sem("b_lo")
        wo_in, wo_mm = sem("wo_in"), sem("wo_mm")
        m_ssq, m_tot, m_sd, m_rs, x1_rdy, x1_st = (
            sem(n) for n in ("m_ssq", "m_tot", "m_sd", "m_rs", "x1_rdy", "x1_st"))
        h2_ssq, h2_sd, h2_rs, h2_norm, h2_tr, h2_hi_rdy, h2_lo_rdy = (
            sem(n) for n in ("h2_ssq", "h2_sd", "h2_rs", "h2_norm", "h2_tr", "h2_hi_rdy", "h2_lo_rdy"))
        gpo_in, x1_in = sem("gpo_in"), sem("x1_in")
        u_silu, u_prod, u_hi, u_lo = sem("u_silu"), sem("u_prod"), sem("u_hi"), sem("u_lo")
        f_mm, f_ssq, f_tot, f_sd, f_rs, y_rdy, y_st = (
            sem(n) for n in ("f_mm", "f_ssq", "f_tot", "f_sd", "f_rs", "y_rdy", "y_st"))

        block = ctx.enter_context(nc.Block())

        def job_emptied(eng, j):
            who = job_engine(*JOBS[j])
            act, dve = JOB_COUNTS[j]
            if who == "act":
                eng.wait_ge(job_act, act)
            else:
                eng.wait_ge(job_dve, dve)

        def job_scale(kind):
            return {"qs": SWA_SCALE, "q": MLA_SCALE}.get(kind, 1.0)

        def job_index(kind, n):
            return JOBS.index((kind, n))

        def rope_out(eng, base, x1v, x2v, cosv, sinv, ta, tb, tc, td, outs):
            eng.tensor_tensor(ta, x1v, cosv, ALU.mult).then_inc(pool_step, 1)
            eng.tensor_tensor(tb, x2v, sinv, ALU.mult).then_inc(pool_step, 1)
            eng.tensor_tensor(tc, x2v, cosv, ALU.mult).then_inc(pool_step, 1)
            eng.tensor_tensor(td, x1v, sinv, ALU.mult).then_inc(pool_step, 1)
            eng.wait_ge(pool_step, base + 4)
            for part, x1o, x2o in outs:
                eng.tensor_tensor(x1o, part(ta), part(tb), ALU.subtract).then_inc(pool_step, 1)
                eng.tensor_tensor(x2o, part(tc), part(td), ALU.add).then_inc(pool_step, 1)
            eng.wait_ge(pool_step, base + 4 + 2 * len(outs))
            return base + 4 + 2 * len(outs)

        Z_ROTATED = 4 + 10 + 6
        Q_ROTATED = Z_ROTATED + 6

        def job_copies(kind, n, bank):
            if kind == "ckv":
                c = slice(n * P, (n + 1) * P)
                return [(ckv_T[:, :, c], bank[:, 0:256].rearrange("p (k n) -> p k n", k=2)), (ks_T[:, c], bank[:, 256:384]),
                        (kpe_T[64:96, c], bank[0:32, 384:512])]
            if kind == "qs":
                if n == 4:
                    return [(qs_Ts[:], bank.rearrange("p (i b t) -> p b i t", i=4, b=STREAMS))]
                return [(qs_T[:, 2 * n:2 * n + 2], bank.rearrange("p (i c n) -> p c i n", i=4, c=2))]
            if kind == "uq":
                t, half = divmod(n, 2)
                return [(q_t[:, t, 4 * half:4 * half + 4, :], bank[:, 0:384].rearrange("p (h n) -> p h n", h=4))]
            if kind == "q":
                t, half = divmod(n, 2)
                h4 = slice(4 * half, 4 * half + 4)
                if t == 4:
                    return [(q_Ts[0:QK, :, h4, :], bank[0:QK, :].rearrange("p (h b t) -> p b h t", h=4, b=STREAMS))]
                return [(q_T[0:QK, h4, t * P:(t + 1) * P], bank[0:QK, :].rearrange("p (h n) -> p h n", h=4))]
            if kind == "cache":
                return [(ckv_Ta[:, :, n, 0:PAST], bank[:, 0:256].rearrange("p (k n) -> p k n", k=2)),
                        (k_Ta[:, n, 0:PAST], bank[:, 256:384]), (kpe_Ta[64:96, n, 0:PAST], bank[0:32, 384:512])]
            if kind == "wuk":
                return [(wuk_T[:, 2 * n:2 * n + 2, :], bank[0:64, :].rearrange("p (h n) -> p h n", h=2))]
            if kind == "qabs":
                ct, half = divmod(n, 2)
                return [(qabs[:, ct, :, 4 * half:4 * half + 4, :],
                         bank.rearrange("p (h b t) -> p b h t", h=4, b=STREAMS))]
            if kind == "kt":
                return [(k_T[0:NOPE, 2 * n, :], bank[0:64, :]), (k_T[0:NOPE, 2 * n + 1, :], bank[64:128, :])]
            return [(v_p[:, n, :], bank[:, :])]

        def o_copies(k, hi):
            kind, a, _, _ = BLOCKS[k]
            bank = ps[:, out_bank(GROUP[k]), :]
            o_s = os_hi if hi else os_lo
            o_m = om_hi if hi else om_lo
            if kind == "swa_p":
                return [(o_s[:, :, a * CHUNK:(a + 1) * CHUNK], bank[:, 0:256].rearrange("p (j n) -> p j n", j=4))]
            if kind == "swa_s":
                v = bank.rearrange("p (j n) -> p j n", j=4)
                return [(o_s[64 * par:64 * par + 64, 2 * g:2 * g + 2, SEQ:TOK], v[64 * g:64 * g + 64, par:4:2, :])
                        for g in range(2) for par in range(2)]
            if kind == "mla_s":
                return [(olat[:, :, :, a * FRAMES:(a + 1) * FRAMES],
                         bank[:, 0:256].rearrange("p (c h t) -> p c h t", c=2, h=HEADS))]
            return [(o_m[:, :, a * P:(a + 1) * P], bank.rearrange("p (j n) -> p j n", j=4))]

        @block.sync
        def _(sp):
            def load(r, src, width):
                dst = raw[:, r, 0:8 * 128] if width == 128 else raw[:, r, 0:2 * width]
                sp.dma_start(dst.rearrange("p (k n) -> p k n", n=width), src).then_inc(w_raw[r], 16)

            def load_x(t):
                sp.dma_start(x_t[:, t, :], x_rows(t)).then_inc(x_in[t], 16)

            load_x(0)
            load_x(1)
            for j in range(2):
                load(j, win_v[:, 2 * j:2 * j + 2, 0:IN_CHUNK], IN_CHUNK)
            for t in range(2, TILES):
                load_x(t)
            for j in range(2, 4):
                load(j, win_v[:, 2 * j:2 * j + 2, 0:IN_CHUNK], IN_CHUNK)
            with sp.Fori(0, 2) as it:
                for j in range(4):
                    sp.wait_ge(w_lo, it * 4 + (j + 1))
                    load(j, win_v[:, 2 * j:2 * j + 2, bass.ds(it * IN_CHUNK + IN_CHUNK, IN_CHUNK)], IN_CHUNK)
            for j in range(4):
                sp.wait_ge(w_lo, 8 + j + 1)
                load(j, win_v[:, :, MIX_COLS + j * P:MIX_COLS + (j + 1) * P], P)
            def store_gates(base, it, j, buf):
                sp.wait_ge(g_out, it * 4 + (base + j + 1))
                sp.dma_start(gates_dram[bass.ds(it * 4 + (base + j), 1)].rearrange("a p n -> (a p) n"),
                             buf[:, j % 2, :]).then_inc(g_st[j % 2], 16)

            with sp.Fori(0, 2) as it:
                for j in range(4):
                    sp.wait_ge(w_lo, it * 4 + (G0 + j + 1))
                    load(j, win_v[:, :, bass.ds(it * 512 + (MIX_COLS + (4 + j) * P), P)], P)
                    store_gates(0, it, j, gate_s)
            sp.wait_ge(job_full, JOBS1)
            sp.dma_start(c_ckv[:], cache_mla_ckv[0].rearrange("b s c -> s b c")).then_inc(cache_in, 16)
            sp.dma_start(c_k[:], cache_swa_k[0].rearrange("b s g d -> s b (g d)")).then_inc(cache_in, 16)
            sp.dma_start(c_v[:], cache_swa_v[0].rearrange("b s g d -> s b (g d)")).then_inc(cache_in, 16)
            sp.dma_start(c_kpe[:], cache_mla_kpe[0].rearrange("b s c -> s b c")).then_inc(cache_in, 16)
            for j in range(8):
                sp.wait_ge(w_lo, G1 + j + 1)
                if j < 4:
                    load(j, win_v[:, :, MIX_COLS + (12 + j) * P:MIX_COLS + (13 + j) * P], P)
                else:
                    load(j % 4, wbr_v[:, :, (j - 4) * P:(j - 3) * P], P)
                store_gates(8, 0, j, gate_s1)
            sp.wait_ge(z_st, 16 * 24)
            sp.wait_ge(w_used, BR0)
            sp.dma_start(ckv_new[:], s_ckv[0].rearrange("b t c -> t b c")).then_inc(new_in, 16)
            sp.dma_start(v_new[:], s_v[0, :, PAST - FRAMES:PAST].rearrange("b t g d -> t b (g d)")).then_inc(new_in, 16)
            sp.wait_ge(pv_done, NB)
            sp.wait_ge(g_st[0], 16 * 8)
            sp.wait_ge(g_st[1], 16 * 8)
            gates_v = gates_dram.rearrange("(b m) p n -> m p b n", b=2)
            for m in range(2):
                sp.dma_start(gate_r[:, m], gates_v[m]).then_inc(g_ld[m], 16)
            for m in range(8):
                sp.wait_ge(w_lo, BR0 + m + 1)
                if m < 4:
                    load(m % 4, wbr_v[:, :, (m + 4) * P:(m + 5) * P], P)
                else:
                    load(m % 4, wout_v[:, 2 * (m - 4):2 * (m - 4) + 2, 0:512], 512)
                if m < 6:
                    sp.wait_ge(b_prod, 2 * (m + 1))
                    sp.dma_start(gate_r[:, m % 2], gates_v[m + 2]).then_inc(g_ld[m % 2], 16)
            sp.wait_ge(w_used, WO0)
            sp.wait_ge(b_lo, 8)
            for t in range(TILES):
                sp.dma_start(x_r[:, t, :], x_rows(t)).then_inc(wo_in, 16)
            sp.dma_start(gpm_b[:], g_post_mix.to_broadcast([P, D])).then_inc(wo_in, 16)
            sp.dma_start(gpf_b[:], g_pre_ffn.to_broadcast([P, D])).then_inc(wo_in, 16)
            for j in range(4):
                sp.wait_ge(w_lo, WO0 + j + 1)
                load(j, wout_v[:, 2 * j:2 * j + 2, 512:1024], 512)
            for j in range(4):
                sp.wait_ge(w_lo, WO0 + 4 + j + 1)
                load(j, wgu_v[:, :, (j // 2) * P + (j % 2) * DFF:(j // 2 + 1) * P + (j % 2) * DFF], P)
            for t in range(TILES):
                sp.wait_ge(x1_rdy, t + 1)
                sp.dma_start(x1_dram[:, t, :], x1[:, t, :]).then_inc(x1_st, 16)
            with sp.Fori(0, 10) as it:
                for j in range(4):
                    sp.wait_ge(w_lo, it * 4 + (GU0 + j + 1))
                    load(j, wgu_v[:, :, bass.ds(it * 256 + (256 + (j // 2) * P + (j % 2) * DFF), P)], P)
            for j in range(4):
                sp.wait_ge(w_lo, GU0 + 40 + j + 1)
                load(j, wdn_v[:, 2 * j:2 * j + 2, 0:512], 512)
            sp.dma_start(gpo_b[:], g_post_ffn.to_broadcast([P, D])).then_inc(gpo_in, 16)
            for u in range(KF - 4):
                if u == 1:
                    sp.wait_ge(w_used, DN0)
                    sp.wait_ge(x1_st, 16 * TILES)
                    sp.dma_start(x1_r[:], x1_dram).then_inc(x1_in, 16)
                sp.wait_ge(w_lo, DN0 + u + 1)
                half, k = divmod(u + 4, KF // 2)
                load(u % 4, wdn_v[:, 2 * k:2 * k + 2, half * 512:(half + 1) * 512], 512)
            for t in range(TILES):
                sp.wait_ge(y_rdy, t + 1)
                sp.dma_start(y_rows(t), f_t[:, t, :]).then_inc(y_st, 16)
            sp.wait_ge(y_st, 16 * TILES)

        @block.gpsimd
        def _(pool):
            pool.memset(eps_c[:], EPS).then_inc(eps_rdy, 1)
            pool.memset(ident[:], 0.0).then_inc(pool_step, 1)
            pool.memset(mask_q[:], 0.0).then_inc(pool_step, 1)
            pool.memset(mask_k[:], 0.0).then_inc(pool_step, 1)
            pool.wait_ge(pool_step, 3)
            pool.affine_select(out=ident[:], in_=ident[:], compare_op=ALU.not_equal, fill=1.0, base=0,
                               pattern=[[-1, P]], channel_multiplier=1).then_inc(const_rdy, 1)
            pool.memset(mask_q[:, 0:CHUNK], 1.0).then_inc(const_rdy, 1)
            pool.memset(mask_k[:, CHUNK:P], -1e30).then_inc(const_rdy, 1)
            pool.wait_ge(wuq_in, 16)
            pool.tensor_copy(wuq_hi[:], wuq_raw[:]).then_inc(pool_step, 1)
            pool.wait_ge(pool_step, 4)
            pool.tensor_tensor(wuq_lo[:], wuq_raw[:], wuq_hi[:].bitcast(F32), ALU.subtract).then_inc(wuq_rdy, 1)
            pool.wait_ge(wuq_rdy, 1)
            pool.wait_ge(sink_in, 16)
            pool.tensor_copy(sink_s[:], sink_b[0:1, :].unsqueeze(2).to_broadcast([1, HEADS, FRAMES])).then_inc(sink_rdy, 1)
            pool.memset(one_c[:], 1.0).then_inc(sink_rdy, 1)
            pool.wait_ge(bank_empty, 15)
            pool.wait_ge(tab_in, 16 * 4)
            pool.tensor_copy(v_s[:], z[:, :, C_VS:MIX_COLS]).then_inc(v_s_rdy, 1)
            qk = z[:, :, C_QS:C_VS].rearrange("p t (h d) -> p t h d", d=HD)
            pairs = z[:, :, C_QS:C_KS].rearrange("p t (i g d) -> p t i g d", i=4, g=2)
            qk_outs = [(lambda v, g=g: v[:, :, 4 * g:4 * g + 4, :], pairs[:, :, :, g, 0:32], pairs[:, :, :, g, 32:64])
                       for g in range(2)]
            qk_outs.append((lambda v: v[:, :, 8:10, :], qk[:, :, 8:10, 0:32], qk[:, :, 8:10, 32:64]))
            cos_b = cos_t[:].unsqueeze(2).to_broadcast([P, TILES, 10, 32])
            sin_b = sin_t[:].unsqueeze(2).to_broadcast([P, TILES, 10, 32])
            n = rope_out(pool, 4, qk[:, :, :, 0:32], qk[:, :, :, 32:64], cos_b, sin_b,
                         rope_a[:], rope_b[:], rope_c[:], rope_d[:], qk_outs)
            pe_v = z[:, :, C_PE:C_QS]
            n = rope_out(pool, n, pe_v[:, :, 0:16], pe_v[:, :, 16:32], cos_t[:, :, 0:32:2], sin_t[:, :, 0:32:2],
                         rope_a[:, :, 0, 0:16], rope_b[:, :, 0, 0:16], rope_c[:, :, 0, 0:16], rope_d[:, :, 0, 0:16],
                         [(lambda v: v, pe_v[:, :, 0:16], pe_v[:, :, 16:32])])
            pool.wait_ge(z_norm, 2 * TILES)
            def out(dst, src):
                pool.dma_start(dst, src).then_inc(z_st, 16)

            out(p_ckv[0, 0].rearrange("(t p) c -> p t c", p=P), z[:, 0:4, C_KV:C_PE])
            out(s_ckv[0].rearrange("b t c -> (b t) c"), z[:, 4, C_KV:C_PE])
            out(p_kpe[0, 0].rearrange("(t p) c -> p t c", p=P), z[:, 0:4, C_PE:C_QS])
            out(s_kpe[0].rearrange("b t c -> (b t) c"), z[:, 4, C_PE:C_QS])
            out(p_k[0, 0].rearrange("s g d -> s (g d)"), z[:, 3, C_KS:C_VS])
            out(p_v[0, 0].rearrange("s g d -> s (g d)"), z[:, 3, C_VS:MIX_COLS])
            for b in range(STREAMS):
                rows = slice(b * FRAMES, (b + 1) * FRAMES)
                out(s_k[0, b, PAST - FRAMES:PAST].rearrange("s g d -> s (g d)"), z[rows, 4, C_KS:C_VS])
                out(s_v[0, b, PAST - FRAMES:PAST].rearrange("s g d -> s (g d)"), z[rows, 4, C_VS:MIX_COLS])
            out(s_k[0, :, 0:PAST - FRAMES], cache_swa_k[0, :, FRAMES:PAST])
            out(s_v[0, :, 0:PAST - FRAMES], cache_swa_v[0, :, FRAMES:PAST])
            job_emptied(pool, JOBS1 - 1)
            job_emptied(pool, JOBS1 - 2)
            cos_q = cos_t[:, :, 0:32:2].unsqueeze(2).to_broadcast([P, TILES, HEADS, 16])
            sin_q = sin_t[:, :, 0:32:2].unsqueeze(2).to_broadcast([P, TILES, HEADS, 16])
            n = rope_out(pool, n, q_t[:, :, :, NOPE:NOPE + 16], q_t[:, :, :, NOPE + 16:QK], cos_q, sin_q,
                         qro_a[:], qro_b[:], qro_c[:], qro_d[:],
                         [(lambda v: v, q_t[:, :, :, NOPE:NOPE + 16], q_t[:, :, :, NOPE + 16:QK])])
            for ct in range(2):
                pool.tensor_copy(ckv_Ta[:, ct, :, PAST:KEYS],
                                 ckv_T[:, ct, SEQ:TOK].rearrange("p (b t) -> p b t", t=FRAMES)).then_inc(tails_rdy, 1)
            pool.tensor_copy(k_Ta[:, :, PAST:KEYS], ks_T[:, SEQ:TOK].rearrange("p (b t) -> p b t", t=FRAMES)).then_inc(tails_rdy, 1)
            pool.wait_ge(tails_rdy, 3)
            pool.tensor_copy(kpe_Ta[64:96, :, PAST:KEYS],
                             kpe_T[64:96, SEQ:TOK].rearrange("p (b t) -> p b t", t=FRAMES)).then_inc(tails_rdy, 1)
            pool.wait_ge(w_used, BR0)
            pool.tensor_copy(k_T[64:96, :, :], kpe_T[64:96, 0:SEQ].unsqueeze(1).to_broadcast([32, HEADS, SEQ])).then_inc(kpe_rdy, 1)
            pool.wait_ge(z_st, 16 * 24)

        @block.scalar
        def _(act):
            act.dma_start(gpre_b[:], g_pre_mix.to_broadcast([P, D])).then_inc(gpre_in, 16)
            def split_hi(r, arrived, to=None):
                act.wait_ge(w_raw[r], arrived)
                act.activation(whi[:, r % 2, :] if to is None else to, raw[:, r, :], ACT.Copy).then_inc(w_hi, 1)

            def after_slot(base, it, j):
                s = it * 4 + (base + j)
                act.wait_ge(w_used, s + 1)
                r = (base + j + 2) % 4
                split_hi(r, it * 16 + 16 * ((base + j + 2) // 4 + 1))

            def h_stat(t):
                act.wait_ge(x_in[t], 16)
                if t:
                    act.wait_ge(h_ssq, t)
                act.activation(junk_h[:], x_t[:, t, :], ACT.Square, accum_out=ssq_h[:, t:t + 1]).then_inc(h_ssq, 1)
                act.wait_ge(h_ssq, t + 1)
                act.activation(sd_h[:, t:t + 1], ssq_h[:, t:t + 1], ACT.Sqrt, scale=1.0 / D,
                               bias=eps_c[:, 0:1]).then_inc(h_sd, 1)

            act.wait_ge(eps_rdy, 1)
            act.wait_ge(pad_rdy, 1)
            h_stat(0)
            split_hi(0, 16)
            split_hi(1, 16)
            for t in range(TILES):
                if t + 1 < TILES:
                    h_stat(t + 1)
                if t in (2, 3):
                    split_hi(t, 16, in_hi[:, t - 2, :])
                for n in (2 * t, 2 * t + 1):
                    half = n % 2
                    act.wait_ge(h_tr, n + 1)
                    act.activation(h_hi[:, 4 * half:4 * half + 4, t * P:(t + 1) * P],
                                   ps[:, 5 + n % 3, :].rearrange("p (k n) -> p k n", k=4), ACT.Copy).then_inc(h_hi_rdy, 1)
            act.dma_start(wuq_raw[:], w_uq[0].rearrange("(k p) n -> p k n", p=P)).then_inc(wuq_in, 16)
            act.dma_start(cos_t[:], cos_dram.rearrange("p (t c) -> p t c", t=TILES)).then_inc(tab_in, 16)
            act.dma_start(sin_t[:], sin_dram.rearrange("p (t c) -> p t c", t=TILES)).then_inc(tab_in, 16)
            act.dma_start(gq_b[:], g_q.to_broadcast([P, QL])).then_inc(tab_in, 16)
            act.dma_start(gkv_b[:], g_kv.to_broadcast([P, KVL])).then_inc(tab_in, 16)
            for k in range(2):
                act.dma_start(w_uk[:, k], w_ukv[0, k * P:(k + 1) * P, :, 0:NOPE]).then_inc(wukv_in, 16)
                act.dma_start(w_uv[:, k], w_ukv[0, k * P:(k + 1) * P, :, NOPE:NOPE + VDIM]).then_inc(wukv_in, 16)
            act.dma_start(sink_b[:], swa_sinks.to_broadcast([P, HEADS])).then_inc(sink_in, 16)
            for j in range(2):
                act.wait_ge(w_used, j + 1)
                split_hi(j, 32)
            with act.Fori(0, 2) as it:
                for j in range(4):
                    after_slot(4, it, j)
            act.wait_ge(bank_empty, 15)
            for i, (lo, width) in enumerate(((0, QL), (QL, KVL))):
                for t in range(TILES):
                    if i or t:
                        act.wait_ge(z_ssq, i * TILES + t)
                    act.activation(junk_h[:, 0:width], z[:, t, lo:lo + width], ACT.Square,
                                   accum_out=ssq_z[:, i, t:t + 1]).then_inc(z_ssq, 1)
            for i, width in enumerate((QL, KVL)):
                act.wait_ge(z_ssq, 2 * TILES)
                act.activation(sd_z[:, i, 0:TILES], ssq_z[:, i, 0:TILES], ACT.Sqrt, scale=1.0 / width,
                               bias=eps_c[:, 0:1]).then_inc(z_sd, 1)

            def exps(i):
                p0, p1, lo = score_place(i)
                act.wait_ge(s_nm, i + 1)
                if i >= 4:
                    act.wait_ge(pt_full, i - 3)
                act.activation(probs[:, i % 4, lo:lo + p1 - p0], ps[:, score_bank(i), p0:p1], ACT.Exp, bias=nm_c[:, i % 8:i % 8 + 1],
                               accum_out=sum_c[:, i % 8:i % 8 + 1]).then_inc(s_exp, 1)

            def pt_copy(k):
                kind, a, _, _ = BLOCKS[k]
                nk = n_keys(BLOCKS[k])
                full = -(-nk // P) * P if kind in ("swa_p", "mla_p") else P
                rows = CHUNK if kind == "swa_p" and nk % P else P
                act.wait_ge(pt_full, k + 1)
                if k >= 2:
                    act.wait_ge(pv_done, k - 1)
                bank = ps[:, turn_bank(k), :]
                if kind == "swa_p" and rows == CHUNK:
                    if full > P:
                        act.activation(probs_T[:, k % 2, 0:full - P], bank[:, 0:full - P], ACT.Copy)
                    act.activation(probs_T[0:CHUNK, k % 2, full - P:full], bank[0:CHUNK, full - P:full],
                                   ACT.Copy).then_inc(pt_rdy, 1)
                elif kind in ("swa_p", "mla_p"):
                    act.activation(probs_T[:, k % 2, 0:full], bank[:, 0:full], ACT.Copy).then_inc(pt_rdy, 1)
                else:
                    act.activation(probs_T[:, k % 2, 0:P], bank[:, 0:P], ACT.Copy)
                    act.activation(probs_T[0:FRAMES, k % 2, P:2 * P], bank[0:FRAMES, P:2 * P],
                                   ACT.Copy).then_inc(pt_rdy, 1)

            def o_evac(k):
                g = GROUP[k]
                act.wait_ge(pv_done, k + 1)
                copies = o_copies(k, True)
                for dst, src in copies:
                    ins = act.activation(dst, src, ACT.Copy)
                ins.then_inc(o_hi, 1)

            def logits_out(base, it, j, buf):
                act.wait_ge(w_used, it * 4 + (base + j + 1))
                b = 2 * (j % 2)
                act.activation(buf[:, j % 2, :].rearrange("p (n c) -> p n c", n=2), ps[:, b:b + 2, 0:HALF],
                               ACT.Copy).then_inc(g_out, 1)
                after_slot(base, it, j)

            def job(j):
                kind, n = JOBS[j]
                bank = ps[:, job_bank(j), :]
                who = job_engine(kind, n)
                if who == "dve":
                    return
                act.wait_ge(job_full, j + 1)
                if kind == "qlat":
                    act.activation(ql_hi[:, :, n * P:(n + 1) * P], bank[:, 0:384].rearrange("p (k n) -> p k n", k=3),
                                   ACT.Copy).then_inc(job_act, 1)
                else:
                    copies = job_copies(kind, n, bank)
                    for dst, src in copies:
                        ins = act.activation(dst, src, ACT.Copy, scale=job_scale(kind))
                    ins.then_inc(job_act, 1)

            for j in range(8):
                if j >= 2:
                    act.wait_ge(g_st[j % 2], 16 * (j // 2))
                logits_out(G0, 0, j, gate_s)
            for j in range(JOBS1):
                job(j)
            for i in range(NA + 2):
                if i >= 2 and LAST_OF[i - 2]:
                    o_evac(i - 2)
                if i < NA:
                    exps(i)
                if 1 <= i <= NA:
                    pt_copy(i - 1)
                if i % 4 == 1 and i > 1:
                    a = i // 4 - 1
                    act.wait_ge(g_st[a % 2], 64 + 16 * (a // 2))
                    logits_out(G1, 0, a, gate_s1)
            for j in range(JOBS1, len(JOBS)):
                if JOBS[j] == ("wuk", 0):
                    for u in range(2):
                        act.wait_ge(g_st[u], 16 * 8)
                job(j)

            for i in range(NA, NB + 6):
                if i < NB:
                    exps(i)
                if i >= NA + 6 and LAST_OF[i - 6]:
                    o_evac(i - 6)
                if NA + 3 <= i < NB + 3:
                    pt_copy(i - 3)
            act.wait_ge(pv_done, NB + 1)
            act.activation(om_hi[:, :, SEQ:TOK], ps[:, VALUE_BANK, :].rearrange("p (h n) -> p h n", h=4),
                           ACT.Copy).then_inc(o_hi, 1)

            with act.Fori(0, 2) as it:
                for j in range(4):
                    act.wait_ge(g_ld[j % 2], it * 32 + 16 * (j // 2 + 1))
                    act.activation(gate_r[:, j % 2], gate_r[:, j % 2], ACT.Sigmoid).then_inc(g_sig, 1)
                    after_slot(BR0, it, j)
                    act.wait_ge(b_sum, it * 4 + (j + 1))
                    act.activation(m_hi[:, bass.ds(it * 4 + j, 1), :].rearrange("p a n -> p (a n)"),
                                   mix_s[:, j % 2, :], ACT.Copy).then_inc(b_hi, 1)
            after_slot(WO0, 0, 0)
            after_slot(WO0, 0, 1)
            act.wait_ge(b_lo, 8)
            for j in range(4):
                split_hi(j, 16 * ((WO0 + 4 + j) // 4 + 1), wo_hi[:, j, :])

            def wo_square(half, t):
                if t < TILES - 1:
                    act.wait_ge(wo_mm, 4 * half + t + 1)
                else:
                    act.wait_ge(w_used, WO0 + 4 * half + 4)
                if half or t:
                    act.wait_ge(m_ssq, 5 * half + t)
                act.activation(junk_m[:, 0:512], ps[:, t, :], ACT.Square, accum_out=ssq_a[:, half, t:t + 1]).then_inc(m_ssq, 1)

            for t in range(TILES):
                wo_square(0, t)
            act.wait_ge(w_used, WO0 + 4)
            split_hi(0, 16 * (GU0 // 4 + 1))
            split_hi(1, 16 * (GU0 // 4 + 1))

            def h2_hi_copies(t):
                for half in range(2):
                    n = 2 * t + half
                    act.wait_ge(h2_tr, n + 1)
                    act.activation(h2_hi[:, 4 * half:4 * half + 4, t * P:(t + 1) * P],
                                   ps[:, 5 + n % 3, :].rearrange("p (k n) -> p k n", k=4), ACT.Copy).then_inc(h2_hi_rdy, 1)

            for t in range(TILES):
                wo_square(1, t)
                act.wait_ge(m_tot, t + 1)
                act.activation(rs_a[:, 1, t:t + 1], rs_a[:, 0, t:t + 1], ACT.Sqrt, scale=1.0 / D,
                               bias=eps_c[:, 0:1]).then_inc(m_sd, 1)
                if t:
                    h2_hi_copies(t - 1)
                act.wait_ge(x1_rdy, t + 1)
                act.wait_ge(m_ssq, TILES + t + 1)
                if t:
                    act.wait_ge(h2_ssq, t)
                act.activation(junk_m[:], x1[:, t, :], ACT.Square, accum_out=ssq_h[:, t:t + 1]).then_inc(h2_ssq, 1)
                act.wait_ge(h2_ssq, t + 1)
                act.activation(sd_h[:, t:t + 1], ssq_h[:, t:t + 1], ACT.Sqrt, scale=1.0 / D,
                               bias=eps_c[:, 0:1]).then_inc(h2_sd, 1)
            h2_hi_copies(TILES - 1)
            act.wait_ge(x1_st, 16 * TILES)
            with act.Fori(0, 11) as it:
                for q in range(2):
                    after_slot(GU0, it, 2 * q)
                    act.activation(silu_s[:, q, :].rearrange("p (n c) -> p n c", n=2), ps[:, 4 * q:4 * q + 2, 0:HALF],
                                   ACT.Silu).then_inc(u_silu, 1)
                    after_slot(GU0, it, 2 * q + 1)
                    act.wait_ge(u_prod, it * 2 + (q + 1))
                    act.activation(gu_hi[:, bass.ds(it * 2 + q, 1), :].rearrange("p a n -> p (a n)"), gu_s[:, q, :],
                                   ACT.Copy).then_inc(u_hi, 1)
            def f_square(half, t):
                if t < TILES - 1:
                    act.wait_ge(f_mm, 4 * half + t + 1)
                else:
                    act.wait_ge(w_used, DN0 + (half + 1) * (KF // 2))
                if half or t:
                    act.wait_ge(f_ssq, 5 * half + t)
                act.activation(junk_f[:, 0:512], ps[:, (F_BANK[half] + t) % 8, :], ACT.Square, accum_out=ssq_z[:, half, t:t + 1]).then_inc(f_ssq, 1)

            for u in range(KF - 2):
                if u == KF // 2 - 1:
                    for t in range(TILES):
                        f_square(0, t)
                act.wait_ge(w_used, DN0 + min(u + 1, KF - 3))
                s2 = DN0 + u + 2
                split_hi(s2 % 4, 16 * (s2 // 4 + 1), dn_hi[:, 0, :] if s2 == SLOTS - 1 else None)
            for t in range(TILES):
                f_square(1, t)
                act.wait_ge(f_tot, t + 1)
                act.activation(sd_z[:, 1, t:t + 1], sd_z[:, 0, t:t + 1], ACT.Sqrt, scale=1.0 / D,
                               bias=eps_c[:, 0:1]).then_inc(f_sd, 1)

        @block.tensor
        def _(pe):
            def mm3(out, left, right, first, last):
                pe.matmul(out, left[1], right[0], start=first, stop=False)
                pe.matmul(out, left[0], right[1], start=False, stop=False)
                return pe.matmul(out, left[0], right[0], start=False, stop=last)

            def wide(r, act_hi, act_lo, banks, k0, k1, n_k, w0=0):
                for k in range(k0, k1):
                    for n, bank in enumerate(banks):
                        w = slice((w0 + k) * P, (w0 + k + 1) * P)
                        rows = slice(n * HALF, (n + 1) * HALF)
                        ins = mm3(ps[:, bank, 0:HALF], (whi[:, r, w], wlo[:, r, w]),
                                  (act_hi[:, k, rows], act_lo[:, k, rows]), k == 0, k == n_k - 1)
                return ins

            def wide_half(r, act_hi, act_lo, bank, n, k0, k1):
                rows = slice(n * HALF, (n + 1) * HALF)
                for k in range(k0, k1):
                    w = slice(k * P, (k + 1) * P)
                    ins = mm3(ps[:, bank, 0:HALF], (whi[:, r, w], wlo[:, r, w]),
                              (act_hi[:, k, rows], act_lo[:, k, rows]), k == 0, k == KD - 1)
                return ins

            def tall(s_wait, r, width, a_hi, a_lo, k0, k_last, bank_wait, mm_sem, bank0=0, w_hi_at=whi, w_lo_at=wlo):
                pe.wait_ge(w_lo, s_wait)
                for kk in range(2):
                    k = k0 + kk
                    for t in range(TILES):
                        if k == 0 and bank_wait is not None:
                            bank_wait(t)
                        w = slice(kk * width, (kk + 1) * width)
                        rows = slice(t * P, (t + 1) * P)
                        ins = mm3(ps[:, (bank0 + t) % 8, 0:width], (a_hi[:, k, rows], a_lo[:, k, rows]),
                                  (w_hi_at[:, r, w], w_lo_at[:, r, w]), k == 0, k == k_last)
                        if k == k_last and t < TILES - 1:
                            ins.then_inc(mm_sem, 1)
                ins.then_inc(w_used, 1)

            def h_turn(t):
                pe.wait_ge(h_norm, t + 1)
                for n in (2 * t, 2 * t + 1):
                    if n >= 3:
                        pe.wait_ge(h_lo_rdy, n - 2)
                    for k in range(4):
                        c = (4 * (n % 2) + k) * P
                        ins = pe.transpose(ps[:, 5 + n % 3, k * P:(k + 1) * P], x_t[:, t, c:c + P], ident[:])
                    ins.then_inc(h_tr, 1)

            pe.wait_ge(const_rdy, 3)
            h_turn(0)
            for t in range(TILES):
                if t + 1 < TILES:
                    h_turn(t + 1)
                pe.wait_ge(h_lo_rdy, 2 * t + 2)
                rows = slice(t * P, (t + 1) * P)
                for k in range(4):
                    j, kk = divmod(k, 2)
                    if t == 0:
                        pe.wait_ge(w_lo, j + 1)
                    w = slice(kk * IN_CHUNK, (kk + 1) * IN_CHUNK)
                    ins = mm3(ps[:, t, 0:IN_CHUNK], (h_hi[:, k, rows], h_lo[:, k, rows]),
                              (whi[:, j, w], wlo[:, j, w]), k == 0, False)
                    if t == TILES - 1 and kk == 1:
                        ins.then_inc(w_used, 1)
            for j in (2, 3):
                tall(j + 1, j % 2, IN_CHUNK, h_hi, h_lo, 2 * j, KD - 1, None, z_mm, 0, in_hi, in_lo)
            with pe.Fori(0, 2) as it:
                for j in range(4):
                    tall(it * 4 + (4 + j + 1), j % 2, IN_CHUNK, h_hi, h_lo, 2 * j, KD - 1,
                         lambda t: pe.wait_ge(bank_empty, it * 5 + (t + 1)), z_mm)

            pe.wait_ge(bank_empty, 15)
            with pe.Fori(0, 2) as it:
                for j in range(4):
                    pe.wait_ge(w_lo, it * 4 + (G0 + j + 1))
                    b = 2 * (j % 2)
                    wide(j % 2, h_hi, h_lo, (b, b + 1), 0, KD, KD).then_inc(w_used, 1)

            def job(j):
                kind, n = JOBS[j]
                bank = ps[:, job_bank(j), :]
                if 4 <= j < JOBS1 or j >= JOBS1 + 4:
                    job_emptied(pe, j - 4)
                c = slice(n * P, (n + 1) * P)
                if kind == "qlat":
                    for i in range(3):
                        ins = pe.transpose(bank[:, i * P:(i + 1) * P], z[:, n, i * P:(i + 1) * P], ident[:])
                elif kind == "ckv":
                    for i, c0 in enumerate((C_KV, C_KV + P, C_KS)):
                        pe.transpose(bank[:, i * P:(i + 1) * P], z[:, n, c0:c0 + P], ident[:])
                    ins = pe.transpose(bank[0:32, 384:512], z[:, n, C_PE:C_QS], ident[:])
                elif kind == "qs":
                    for i in range(4):
                        c0 = C_QS + i * P
                        ins = pe.transpose(bank[:, i * P:(i + 1) * P], z[:, n, c0:c0 + P], ident[:])
                elif kind == "uq":
                    t, half = divmod(n, 2)
                    job_emptied(pe, job_index("qlat", t))
                    if n == 0:
                        pe.wait_ge(wuq_rdy, 1)
                        pe.wait_ge(z_st, 16 * 24)
                    rows = slice(t * P, (t + 1) * P)
                    cols = slice(384 * half, 384 * half + 384)
                    for k in range(3):
                        ins = mm3(bank[:, 0:384], (ql_hi[:, k, rows], ql_lo[:, k, rows]),
                                  (wuq_hi[:, k, cols], wuq_lo[:, k, cols]), k == 0, k == 2)
                elif kind == "q":
                    t, half = divmod(n, 2)
                    if n == 0:
                        pe.wait_ge(pool_step, Q_ROTATED)
                    for i in range(4):
                        ins = pe.transpose(bank[0:QK, i * P:(i + 1) * P], q_t[:, t, 4 * half + i, :], ident[:])
                elif kind == "cache":
                    pe.wait_ge(cache_in, 16 * 4)
                    for i in range(2):
                        pe.transpose(bank[:, i * P:(i + 1) * P], c_ckv[:, n, i * P:(i + 1) * P], ident[:])
                    pe.transpose(bank[:, 256:384], c_k[:, n, :], ident[:])
                    ins = pe.transpose(bank[0:32, 384:512], c_kpe[:, n, :], ident[:])
                elif kind == "wuk":
                    pe.wait_ge(wukv_in, 16 * 4)
                    for i in range(2):
                        for ct in range(2):
                            ins = pe.transpose(bank[0:64, (2 * i + ct) * P:(2 * i + ct + 1) * P],
                                               w_uk[:, ct, 2 * n + i, :], ident[:])
                elif kind == "qabs":
                    ct, half = divmod(n, 2)
                    if n == 0:
                        for i in range(4):
                            job_emptied(pe, job_index("wuk", i))
                        job_emptied(pe, job_index("q", 8))
                        job_emptied(pe, job_index("q", 9))
                    for i in range(4):
                        h = 4 * half + i
                        ins = pe.matmul(bank[:, i * P:(i + 1) * P], wuk_T[:, h, ct * P:(ct + 1) * P],
                                        q_Ts[0:NOPE, :, h, :], start=True, stop=True)
                elif kind == "kt":
                    for ct in range(2):
                        ins = pe.matmul(bank[:, :], w_uk[:, ct, 2 * n:2 * n + 2, :], ckv_T[:, ct, 0:SEQ],
                                        start=(ct == 0), stop=(ct == 1))
                else:
                    for ct in range(2):
                        ins = pe.matmul(bank[:, :], ckv_T[:, ct, c], w_uv[:, ct, :, :],
                                        start=(ct == 0), stop=(ct == 1))
                ins.then_inc(job_full, 1)

            def scores(i):
                kind, a, b, c = BLOCKS[i]
                out = ps[:, score_bank(i), :]
                nk = n_keys(BLOCKS[i])
                back = 2 if i < NA else 4
                if i >= back:
                    pe.wait_ge(s_exp, i - back + 1)
                if kind == "swa_p":
                    base, lo, hi = window(a)
                    rows = slice(64 * b, 64 * b + 64)
                    p0, p1, _ = score_place(i)
                    ins = pe.matmul(out[:, p0:p1 - 1], qs_T[rows, a, 2 * c:2 * c + 2, :],
                                    ks_T[rows, base + lo:base + hi], start=True, stop=True)
                elif kind == "swa_s":
                    for g in range(2):
                        rows = slice(64 * g, 64 * g + 64)
                        pe.matmul(out[rows, 0:KEYS], qs_Ts[rows, a, :, :], k_Ta[rows, a, :], start=True, stop=True)
                    ins = pe.matmul(out[:, KEYS:KEYS + 1], sink_s[:].rearrange("p h n -> p (h n)"), one_c[:, 0:1],
                                    start=True, stop=True)
                elif kind == "mla_s":
                    for ct in range(2):
                        pe.matmul(out[:, 0:KEYS], qabs[:, ct, a, :, :], ckv_Ta[:, ct, a, :], start=(ct == 0), stop=False)
                    ins = pe.matmul(out[:, 0:KEYS], q_Ts[64:96, a, :, :],
                                    kpe_Ta[64:96, a, :], start=False, stop=True)
                else:
                    h = 2 * b + c
                    pe.matmul(out[:, 0:nk], q_T[0:QK, h, a * P:(a + 1) * P], k_T[0:QK, h, 0:nk], start=True, stop=False)
                    ins = pe.matmul(out[:, a * P:nk], mask_q[:], mask_k[:], start=False, stop=True)
                ins.then_inc(s_full, 1)

            def turn(k):
                kind, a, _, _ = BLOCKS[k]
                nk = n_keys(BLOCKS[k])
                pe.wait_ge(s_norm, k + 1)
                back = 1 if k < NA else 2
                if k >= back:
                    pe.wait_ge(pt_rdy, k - back + 1)
                for i in range(-(-nk // P)):
                    n = min(P, nk - i * P)
                    ins = pe.transpose(ps[0:n, turn_bank(k), i * P:(i + 1) * P], probs[:, k % 4, i * P:i * P + n], ident[:])
                ins.then_inc(pt_full, 1)

            def outputs(k):
                kind, a, b, c = BLOCKS[k]
                g = GROUP[k]
                bank = ps[:, out_bank(g), :]
                pt = probs_T[:, k % 2, :]
                pe.wait_ge(pt_rdy, k + 1)
                before = last_in_bank(g)
                if FIRST_OF[k] and before is not None:
                    pe.wait_ge(o_hi, before + 1)
                    pe.wait_ge(o_lo, lo_groups(before + 1))
                if kind == "swa_p":
                    base, lo, hi = window(a)
                    pieces = []
                    for i in range(-(-hi // P)):
                        p0, p1 = max(lo - i * P, 0), min(hi - i * P, P)
                        pieces.append((base // P + i, i, p0, p1))
                    for u in range(2):
                        for n, (kt, i, p0, p1) in enumerate(pieces):
                            ins = pe.matmul(bank[64 * u:64 * u + 64, (2 * b + c) * CHUNK:(2 * b + c + 1) * CHUNK],
                                            v_s[p0:p1, kt, 64 * b:64 * b + 64],
                                            pt[p0:p1, i * P + 64 * u:i * P + 64 * u + 64],
                                            start=(n == 0), stop=(n == len(pieces) - 1))
                elif kind == "swa_s":
                    o = bank.rearrange("p (j n) -> p j n", j=4)
                    for gg in range(2):
                        rows = slice(64 * gg, 64 * gg + 64)
                        to = o[rows, :, a * FRAMES:(a + 1) * FRAMES]
                        pe.matmul(to, c_v[:, a, rows], pt[:, rows], start=True, stop=False)
                        ins = pe.matmul(to, v_new[:, a, rows], pt[0:FRAMES, P + 64 * gg:P + 64 * gg + 64],
                                        start=False, stop=True)
                elif kind == "mla_s":
                    for ct in range(2):
                        cc = slice(ct * P, (ct + 1) * P)
                        pe.matmul(bank[:, cc], c_ckv[:, a, cc], pt[:, 0:P], start=True, stop=False)
                        ins = pe.matmul(bank[:, cc], ckv_new[:, a, cc], pt[0:FRAMES, P:2 * P], start=False, stop=True)
                else:
                    h = 2 * b + c
                    for i in range(a + 1):
                        ins = pe.matmul(bank[64 * c:64 * c + 64, b * P:(b + 1) * P], v_p[:, i, 64 * h:64 * h + 64],
                                        pt[:, i * P:(i + 1) * P], start=(i == 0), stop=(i == a))
                ins.then_inc(pv_done, 1)

            pe.wait_ge(pool_step, Z_ROTATED)
            pe.wait_ge(z_norm, 2 * TILES)
            for j in range(JOBS1):
                job(j)
            job_emptied(pe, JOBS1 - 2)
            job_emptied(pe, JOBS1 - 1)
            pe.wait_ge(v_s_rdy, 1)
            pe.wait_ge(sink_rdy, 2)
            pe.wait_ge(probs_rdy, 3)
            for i in range(NA + 1):
                a, n = divmod(i, 4)
                b = 2 * (a % 2)
                if i < NA:
                    if n == 0:
                        pe.wait_ge(w_lo, G1 + a + 1)
                    scores(i)
                    wide(a % 2, h_hi, h_lo, (b, b + 1), 2 * n, 2 * n + 1, KD)
                if i:
                    turn(i - 1)
                if i < NA:
                    ins = wide(a % 2, h_hi, h_lo, (b, b + 1), 2 * n + 1, 2 * n + 2, KD)
                    if n == 3:
                        ins.then_inc(w_used, 1)
                if i:
                    outputs(i - 1)
            for j in range(JOBS1, len(JOBS)):
                if j == JOBS1:
                    pe.wait_ge(g_out, 15)
                elif j == JOBS1 + 2:
                    pe.wait_ge(g_out, 16)
                job(j)

            pe.wait_ge(o_hi, SEQ // CHUNK)
            pe.wait_ge(o_lo, SEQ // CHUNK)
            for j in range(len(JOBS) - 6, len(JOBS) - 2):
                job_emptied(pe, j)
            pe.wait_ge(kpe_rdy, 1)
            pe.wait_ge(tails_rdy, 4)
            pe.wait_ge(new_in, 32)

            for i in range(NA, NB + 5):
                if i < NA + 2:
                    job_emptied(pe, len(JOBS) - 2 + i - NA)
                if i < NB:
                    scores(i)
                if NA + 3 <= i < NB + 3:
                    turn(i - 3)
                if i >= NA + 5:
                    outputs(i - 5)
            pe.wait_ge(o_hi, NGROUPS - 1)
            pe.wait_ge(o_lo, lo_groups(NGROUPS - 1))
            for h in range(HEADS):
                for ct in range(2):
                    ins = pe.matmul(ps[64 * (h % 2):64 * (h % 2) + 64, VALUE_BANK, (h // 2) * P:(h // 2 + 1) * P],
                                    w_uv[:, ct, h, :], olat[:, ct, h, :], start=(ct == 0), stop=(ct == 1))
            ins.then_inc(pv_done, 1)
            with pe.Fori(0, 2) as it:
                for j in range(4):
                    pe.wait_ge(w_lo, it * 4 + (BR0 + j + 1))
                    b = 4 * (j % 2)
                    wide(j % 2, os_hi, os_lo, (b + 2, b + 3), 0, 4, 4, 4)
                    if j == 0:
                        pe.wait_ge(o_hi, NGROUPS + 1)
                        pe.wait_ge(o_lo, lo_groups(NGROUPS) + 1)
                    wide(j % 2, om_hi, om_lo, (b, b + 1), 0, 4, 4).then_inc(w_used, 1)

            for j in range(4):
                pe.wait_ge(b_lo, 2 * (j + 1))
                tall(WO0 + j + 1, j % 2, 512, m_hi, m_lo, 2 * j, KD - 1,
                     lambda t: pe.wait_ge(b_prod, 14 if t < 4 else 16), wo_mm)

            def h2_turn(t):
                pe.wait_ge(h2_norm, t + 1)
                for half in range(2):
                    n = 2 * t + half
                    if n >= 3:
                        pe.wait_ge(h2_lo_rdy, n - 2)
                    for k in range(4):
                        c = (4 * half + k) * P
                        ins = pe.transpose(ps[:, 5 + n % 3, k * P:(k + 1) * P], x_r[:, t, c:c + P], ident[:])
                    ins.then_inc(h2_tr, 1)

            for t in range(TILES):
                pe.wait_ge(bank_empty, 15 + t + 1)
                rows = slice(t * P, (t + 1) * P)
                for k in range(KD):
                    j, kk = divmod(k, 2)
                    if t == 0:
                        pe.wait_ge(w_lo, WO0 + 4 + j + 1)
                    w = slice(kk * 512, (kk + 1) * 512)
                    ins = mm3(ps[:, t, :], (m_hi[:, k, rows], m_lo[:, k, rows]), (wo_hi[:, j, w], wo_lo[:, j, w]),
                              k == 0, k == KD - 1)
                    if t == TILES - 1 and kk == 1:
                        ins.then_inc(w_used, 1)
                if t < TILES - 1:
                    ins.then_inc(wo_mm, 1)
                if t:
                    h2_turn(t - 1)
            pe.wait_ge(w_lo, GU0 + 1)
            pe.wait_ge(h2_lo_rdy, 6)
            pe.wait_ge(bank_empty, 24)
            wide_half(0, h2_hi, h2_lo, 0, 0, 0, KD)
            pe.wait_ge(w_lo, GU0 + 2)
            wide_half(1, h2_hi, h2_lo, 2, 0, 0, KD // 2)
            h2_turn(TILES - 1)
            wide_half(1, h2_hi, h2_lo, 2, 0, KD // 2, KD)
            pe.wait_ge(h2_lo_rdy, 2 * TILES)
            pe.wait_ge(bank_empty, 25)
            wide_half(0, h2_hi, h2_lo, 1, 1, 0, KD).then_inc(w_used, 1)
            wide_half(1, h2_hi, h2_lo, 3, 1, 0, KD).then_inc(w_used, 1)
            for u in (2, 3):
                pe.wait_ge(w_lo, GU0 + u + 1)
                wide(u % 2, h2_hi, h2_lo, (2 * u, 2 * u + 1), 0, KD, KD).then_inc(w_used, 1)
            with pe.Fori(0, 10) as it:
                for u in range(4):
                    pe.wait_ge(w_lo, it * 4 + (GU0 + 4 + u + 1))
                    wide(u % 2, h2_hi, h2_lo, (2 * u, 2 * u + 1), 0, KD, KD).then_inc(w_used, 1)
            def f_bank(half, t):
                if half == 0:
                    pe.wait_ge(u_prod, KF - 1 if t < 4 else KF)
                elif t > 2:
                    pe.wait_ge(bank_empty, 25 + t - 2)

            for u in range(KF - 2):
                half, j = divmod(u, KF // 2)
                if half == 0:
                    pe.wait_ge(u_lo, 2 * (j + 1))
                tall(DN0 + u + 1, u % 2, 512, gu_hi, gu_lo, 2 * j, KF - 1,
                     lambda t, half=half: f_bank(half, t), f_mm, F_BANK[half])
            pe.wait_ge(w_lo, SLOTS)
            for t in range(TILES):
                rows = slice(t * P, (t + 1) * P)
                for k in range(KF - 4, KF):
                    kk = k % 2
                    w = slice(kk * 512, (kk + 1) * 512)
                    first = k < KF - 2
                    right = (whi[:, 0, w], wlo[:, 0, w]) if first else (dn_hi[:, 0, w], dn_lo[:, 0, w])
                    ins = mm3(ps[:, (F_BANK[1] + t) % 8, :], (gu_hi[:, k, rows], gu_lo[:, k, rows]), right,
                              False, k == KF - 1)
                    if t == TILES - 1 and kk == 1:
                        ins.then_inc(w_used, 1)
                if t < TILES - 1:
                    ins.then_inc(f_mm, 1)

        @block.vector
        def _(dve):
            def split_lo(s1, r, hi=whi, lo=wlo, place=None):
                place = r % 2 if place is None else place
                dve.wait_ge(w_hi, s1)
                dve.tensor_tensor(lo[:, place, :], raw[:, r, :], hi[:, place, :].bitcast(F32),
                                  ALU.subtract).then_inc(w_lo, 1)

            def after_slot(base, it, j):
                split_lo(it * 4 + (base + j + 3), (base + j + 2) % 4)

            dve.memset(raw[:, :, 960:1024], 0.0).then_inc(pad_rdy, 1)

            def h_scale(t):
                dve.wait_ge(h_sd, t + 1)
                dve.reciprocal(r_h[:, t:t + 1], sd_h[:, t:t + 1]).then_inc(h_rs, 1)
                dve.wait_ge(h_rs, t + 1)
                dve.scalar_tensor_tensor(out=x_t[:, t, :], in0=x_t[:, t, :], scalar=r_h[:, t:t + 1], in1=gpre_b[:],
                                         op0=ALU.mult, op1=ALU.mult).then_inc(h_norm, 1)

            dve.wait_ge(gpre_in, 16)
            h_scale(0)
            split_lo(1, 0)
            split_lo(2, 1)
            for t in range(TILES):
                if t + 1 < TILES:
                    h_scale(t + 1)
                if t in (2, 3):
                    split_lo(t + 1, t, in_hi, in_lo, t - 2)
                for n in (2 * t, 2 * t + 1):
                    half = n % 2
                    to = slice(4 * half, 4 * half + 4), slice(t * P, (t + 1) * P)
                    dve.wait_ge(h_hi_rdy, n + 1)
                    dve.tensor_tensor(h_lo[:, to[0], to[1]], ps[:, 5 + n % 3, :].rearrange("p (k n) -> p k n", k=4),
                                      h_hi[:, to[0], to[1]].bitcast(F32), ALU.subtract).then_inc(h_lo_rdy, 1)
            split_lo(5, 0)
            split_lo(6, 1)

            def z_out(it, chunk, cols):
                for t in range(TILES):
                    if t < TILES - 1:
                        dve.wait_ge(z_mm, it * 4 + (4 * chunk + t + 1))
                    else:
                        dve.wait_ge(w_used, it * 4 + 4 * (chunk + 1))
                    dve.tensor_copy(z[:, t, cols], ps[:, t, 0:IN_CHUNK]).then_inc(bank_empty, 1)

            z_out(0, 0, slice(0, IN_CHUNK))
            with dve.Fori(0, 2) as it:
                for j in range(4):
                    if j == 3:
                        z_out(it, 1, bass.ds(it * IN_CHUNK + IN_CHUNK, IN_CHUNK))
                    after_slot(4, it, j)
            dve.wait_ge(tab_in, 16 * 4)
            for i, (lo, width, g_b) in enumerate(((0, QL, gq_b), (QL, KVL, gkv_b))):
                dve.wait_ge(z_sd, i + 1)
                dve.reciprocal(r_z[:, i, 0:TILES], sd_z[:, i, 0:TILES]).then_inc(z_rs, 1)
                dve.wait_ge(z_rs, i + 1)
                for t in range(TILES):
                    dve.scalar_tensor_tensor(out=z[:, t, lo:lo + width], in0=z[:, t, lo:lo + width],
                                             scalar=r_z[:, i, t:t + 1], in1=g_b[:],
                                             op0=ALU.mult, op1=ALU.mult).then_inc(z_norm, 1)

            def row_max(i):
                p0, p1, _ = score_place(i)
                dve.wait_ge(s_full, i + 1)
                dve.tensor_reduce(nm_c[:, i % 8:i % 8 + 1], ps[:, score_bank(i), p0:p1], AX_X, ALU.max,
                                  negate=True).then_inc(s_nm, 1)

            def normalise(k):
                kind, a, _, _ = BLOCKS[k]
                nk = n_keys(BLOCKS[k])
                lo = window(a)[1] if kind == "swa_p" else 0
                col = slice(k % 8, k % 8 + 1)
                dve.wait_ge(s_exp, k + 1)
                dve.reciprocal(inv_c[:, col], sum_c[:, col]).then_inc(s_inv, 1)
                dve.wait_ge(s_inv, k + 1)
                dve.tensor_scalar(probs[:, k % 4, lo:nk], probs[:, k % 4, lo:nk], inv_c[:, col], None,
                                  ALU.mult).then_inc(s_norm, 1)

            def o_evac(k):
                g = GROUP[k]
                if GROUP_KIND[g] == "mla_s":
                    return
                dve.wait_ge(o_hi, g + 1)
                for (dst, src), (hi_part, _) in zip(o_copies(k, False), o_copies(k, True)):
                    ins = dve.tensor_tensor(dst, src, hi_part.bitcast(F32), ALU.subtract)
                ins.then_inc(o_lo, 1)

            def job(j):
                kind, n = JOBS[j]
                bank = ps[:, job_bank(j), :]
                who = job_engine(kind, n)
                if who == "act":
                    return
                if kind == "qlat":
                    dve.wait_ge(job_act, JOB_COUNTS[j][0])
                    c = slice(n * P, (n + 1) * P)
                    dve.tensor_tensor(ql_lo[:, :, c], bank[:, 0:384].rearrange("p (k n) -> p k n", k=3),
                                      ql_hi[:, :, c].bitcast(F32), ALU.subtract).then_inc(job_dve, 1)
                    return
                dve.wait_ge(job_full, j + 1)
                for dst, src in job_copies(kind, n, bank):
                    if kind == "q":
                        ins = dve.tensor_scalar(dst, src, job_scale(kind), None, ALU.mult)
                    else:
                        ins = dve.tensor_copy(dst, src)
                ins.then_inc(job_dve, 1)

            with dve.Fori(0, 2) as it:
                for j in range(4):
                    after_slot(G0, it, j)
            for j in range(JOBS1):
                job(j)
            dve.memset(probs[:, :, 0:CHUNK], 0.0).then_inc(probs_rdy, 1)
            dve.wait_ge(sink_in, 16)
            for u in range(2):
                dve.wait_ge(g_st[u], 16 * 4)
            dve.wait_ge(job_act, JOB_COUNTS[JOBS1 - 1][0])
            dve.wait_ge(job_dve, JOB_COUNTS[JOBS1 - 1][1])
            for u in range(2):
                rows = slice(CHUNK * u, CHUNK * (u + 1))
                dve.tensor_copy(ps[rows, 4:6, SINK_AT[0]:SINK_AT[1] + 1:SINK_AT[1] - SINK_AT[0]].rearrange("p c g -> p g c"),
                                sink_b[rows, u:HEADS:2].rearrange("p (g c) -> p g c", g=KV_HEADS)).then_inc(probs_rdy, 1)
            for i in range(NA + 3):
                if 2 <= i < NA + 2 and LAST_OF[i - 2]:
                    o_evac(i - 2)
                if i < NA:
                    row_max(i)
                    normalise(i)
                if i % 4 == 2 and i > 2:
                    after_slot(G1, 0, i // 4 - 1)
            for j in range(JOBS1, len(JOBS)):
                if JOBS[j] == ("wuk", 0):
                    for u in range(2):
                        dve.wait_ge(g_st[u], 16 * 8)
                job(j)

            for i in range(NA, NB + 6):
                if i < NB:
                    row_max(i)
                if NA + 1 <= i < NB + 1:
                    normalise(i - 1)
                if i >= NA + 6 and LAST_OF[i - 6]:
                    o_evac(i - 6)
            dve.wait_ge(o_hi, NGROUPS + 1)
            dve.tensor_tensor(om_lo[:, :, SEQ:TOK], ps[:, VALUE_BANK, :].rearrange("p (h n) -> p h n", h=4),
                              om_hi[:, :, SEQ:TOK].bitcast(F32), ALU.subtract).then_inc(o_lo, 1)

            with dve.Fori(0, 2) as it:
                for j in range(4):
                    m = it * 4 + j
                    dve.wait_ge(w_used, it * 4 + (BR0 + j + 1))
                    dve.wait_ge(g_sig, it * 4 + (j + 1))
                    for b, to in enumerate((mix_a, mix_b)):
                        bank = 4 * (j % 2) + 2 * b
                        dve.tensor_tensor(to[:].rearrange("p (n c) -> p n c", n=2), ps[:, bank:bank + 2, 0:HALF],
                                          gate_r[:, j % 2, b, :].rearrange("p (n c) -> p n c", n=2),
                                          ALU.mult).then_inc(b_prod, 1)
                    dve.wait_ge(b_prod, it * 8 + 2 * (j + 1))
                    dve.tensor_tensor(mix_s[:, j % 2, :], mix_a[:], mix_b[:], ALU.add).then_inc(b_sum, 1)
                    after_slot(BR0, it, j)
                    dve.wait_ge(b_hi, it * 4 + (j + 1))
                    dve.tensor_tensor(m_lo[:, bass.ds(m, 1), :].rearrange("p a n -> p (a n)"), mix_s[:, j % 2, :],
                                      m_hi[:, bass.ds(m, 1), :].rearrange("p a n -> p (a n)").bitcast(F32),
                                      ALU.subtract).then_inc(b_lo, 1)
            after_slot(WO0, 0, 0)
            after_slot(WO0, 0, 1)
            for j in range(4):
                split_lo(WO0 + 4 + j + 1, j, wo_hi, wo_lo, j)
            dve.wait_ge(wo_in, 16 * (TILES + 2))

            def wo_gain(half, t):
                c = slice(half * 512, (half + 1) * 512)
                dve.tensor_tensor(x1[:, t, c], ps[:, t, :], gpm_b[:, c], ALU.mult).then_inc(bank_empty, 1)

            for t in range(TILES):
                dve.wait_ge(m_ssq, t + 1)
                wo_gain(0, t)
            split_lo(GU0 + 1, 0)
            split_lo(GU0 + 2, 1)

            def h2_lo_parts(t):
                for half in range(2):
                    n = 2 * t + half
                    to = slice(4 * half, 4 * half + 4), slice(t * P, (t + 1) * P)
                    dve.wait_ge(h2_hi_rdy, n + 1)
                    dve.tensor_tensor(h2_lo[:, to[0], to[1]], ps[:, 5 + n % 3, :].rearrange("p (k n) -> p k n", k=4),
                                      h2_hi[:, to[0], to[1]].bitcast(F32), ALU.subtract).then_inc(h2_lo_rdy, 1)

            for t in range(TILES):
                c = slice(t, t + 1)
                dve.wait_ge(m_ssq, TILES + t + 1)
                dve.tensor_tensor(rs_a[:, 0, c], ssq_a[:, 0, c], ssq_a[:, 1, c], ALU.add).then_inc(m_tot, 1)
                wo_gain(1, t)
                dve.wait_ge(m_sd, t + 1)
                dve.reciprocal(rs_a[:, 2, c], rs_a[:, 1, c]).then_inc(m_rs, 1)
                dve.wait_ge(m_rs, t + 1)
                dve.wait_ge(bank_empty, 20 + t + 1)
                dve.scalar_tensor_tensor(out=x1[:, t, :], in0=x1[:, t, :], scalar=rs_a[:, 2, c], in1=x_r[:, t, :],
                                         op0=ALU.mult, op1=ALU.add).then_inc(x1_rdy, 1)
                if t:
                    h2_lo_parts(t - 1)
                dve.wait_ge(h2_sd, t + 1)
                dve.reciprocal(r_h[:, c], sd_h[:, c]).then_inc(h2_rs, 1)
                dve.wait_ge(h2_rs, t + 1)
                dve.scalar_tensor_tensor(out=x_r[:, t, :], in0=x1[:, t, :], scalar=r_h[:, c], in1=gpf_b[:],
                                         op0=ALU.mult, op1=ALU.mult).then_inc(h2_norm, 1)
            h2_lo_parts(TILES - 1)
            dve.wait_ge(x1_st, 16 * TILES)
            with dve.Fori(0, 11) as it:
                for q in range(2):
                    after_slot(GU0, it, 2 * q)
                    dve.wait_ge(w_used, it * 4 + (GU0 + 2 * q + 2))
                    dve.wait_ge(u_silu, it * 2 + (q + 1))
                    dve.tensor_tensor(gu_s[:, q, :].rearrange("p (n c) -> p n c", n=2), ps[:, 4 * q + 2:4 * q + 4, 0:HALF],
                                      silu_s[:, q, :].rearrange("p (n c) -> p n c", n=2), ALU.mult).then_inc(u_prod, 1)
                    after_slot(GU0, it, 2 * q + 1)
                    dve.wait_ge(u_hi, it * 2 + (q + 1))
                    f = bass.ds(it * 2 + q, 1)
                    dve.tensor_tensor(gu_lo[:, f, :].rearrange("p a n -> p (a n)"), gu_s[:, q, :],
                                      gu_hi[:, f, :].rearrange("p a n -> p (a n)").bitcast(F32),
                                      ALU.subtract).then_inc(u_lo, 1)
            def f_gain(half, t):
                c = slice(half * 512, (half + 1) * 512)
                dve.tensor_tensor(f_t[:, t, c], ps[:, (F_BANK[half] + t) % 8, :], gpo_b[:, c], ALU.mult).then_inc(bank_empty, 1)

            dve.wait_ge(gpo_in, 16)
            for u in range(KF - 2):
                if u == KF // 2 - 1:
                    for t in range(TILES):
                        dve.wait_ge(f_ssq, t + 1)
                        f_gain(0, t)
                if u < KF - 3:
                    split_lo(DN0 + u + 3, (DN0 + u + 2) % 4)
                else:
                    split_lo(SLOTS, (SLOTS - 1) % 4, dn_hi, dn_lo, 0)
            dve.wait_ge(x1_in, 16)
            for t in range(TILES):
                c = slice(t, t + 1)
                dve.wait_ge(f_ssq, TILES + t + 1)
                dve.tensor_tensor(sd_z[:, 0, c], ssq_z[:, 0, c], ssq_z[:, 1, c], ALU.add).then_inc(f_tot, 1)
                f_gain(1, t)
                dve.wait_ge(f_sd, t + 1)
                dve.reciprocal(r_z[:, 0, c], sd_z[:, 1, c]).then_inc(f_rs, 1)
                dve.wait_ge(f_rs, t + 1)
                dve.wait_ge(bank_empty, 30 + t + 1)
                dve.scalar_tensor_tensor(out=f_t[:, t, :], in0=f_t[:, t, :], scalar=r_z[:, 0, c], in1=x1_r[:, t, :],
                                         op0=ALU.mult, op1=ALU.add).then_inc(y_rdy, 1)


_INS = ["x_prompt", "x_sample", "cache_mla_ckv", "cache_mla_kpe", "cache_swa_k", "cache_swa_v", "g_pre_mix", "w_in",
        "g_q", "w_uq", "g_kv", "w_ukv", "swa_sinks", "w_branch", "w_out", "g_post_mix", "g_pre_ffn", "w_gate_up",
        "w_down", "g_post_ffn"]
_OUTS = [(1, SEQ, D), (STREAMS, FRAMES, D), (1, 1, SEQ, KVL), (1, 1, SEQ, ROPE), (1, 1, PAST, KV_HEADS, HD),
         (1, 1, PAST, KV_HEADS, HD), (1, STREAMS, FRAMES, KVL), (1, STREAMS, FRAMES, ROPE),
         (1, STREAMS, PAST, KV_HEADS, HD), (1, STREAMS, PAST, KV_HEADS, HD)]


def kernel(**inputs):
    import concourse.bacc as _bacc
    from concourse.bass_utils import run_bass_kernel_spmd as _run

    nc = _bacc.Bacc("TRN2", target_bir_lowering=False, num_devices=1)
    arrays, args = {}, []
    for name in _INS:
        a = np.ascontiguousarray(inputs[name])
        arrays[f"in_{name}"] = a
        args.append(nc.dram_tensor(f"in_{name}", a.shape, mybir.dt.from_np(a.dtype), kind="ExternalInput").ap())
    for i, shape in enumerate(_OUTS):
        args.append(nc.dram_tensor(f"out_{i}", shape, F32, kind="ExternalOutput").ap())
    build_layer(nc, *args)
    r = _run(nc, [arrays], core_ids=[0])
    return tuple(r.results[0][f"out_{i}"] for i in range(len(_OUTS)))
```
